# Optimizing a Trainium2 kernel written in Bass

```python
import jax, jax.numpy as jnp
from jax import lax
import numpy as np

D_MODEL = 1024
BATCH = 1
SEQ = 512
DEPTH = 2

F32 = jnp.float32
CTX_LEN = 256
GRID_W = 64
BRANCH_WIDTH = D_MODEL // 2
N_BRANCH = 3
POOL_GROUPS = 4
POOL_WINDOWS = (2, 4, 8, 16)
POOL_WIDTH = BRANCH_WIDTH
POOL_GDIM = POOL_WIDTH // POOL_GROUPS
M_HEADS = 4
M_HDIM = BRANCH_WIDTH // M_HEADS
M_WIDTH = M_HEADS * M_HDIM
M_CHUNK = 128
A_HDIM = 64
A_Q_HEADS = BRANCH_WIDTH // A_HDIM
A_KV_HEADS = A_Q_HEADS // 4
A_GROUP = A_Q_HEADS // A_KV_HEADS
A_Q_WIDTH = A_Q_HEADS * A_HDIM
A_KV_WIDTH = A_KV_HEADS * A_HDIM
WINDOW = 128
A_BLOCK = 128
ROPE_BASE = 10000.0
ROPE_PAIRS = A_HDIM // 4
D_FF = ((8 * D_MODEL + 3 * 256 - 1) // (3 * 256)) * 256
SPLIT_SIZES = (POOL_WIDTH, M_WIDTH, M_WIDTH, M_WIDTH, M_WIDTH, 2 * M_HEADS, 2 * M_HEADS,
               A_Q_WIDTH, A_KV_WIDTH, A_KV_WIDTH, N_BRANCH * D_MODEL)
IN_WIDTH = sum(SPLIT_SIZES)
DN_ALPHA = (2 * DEPTH) ** 0.25
DN_BETA = (8 * DEPTH) ** -0.25
LN_EPS = 1e-5

kernel_name = 'hybrid_pool_mlstm_swa_dit_trunk'

def _layer_norm(x, g=None, b=None):
    xf = x.astype(F32)
    mu = jnp.mean(xf, -1, keepdims=True)
    var = jnp.mean(jnp.square(xf - mu), -1, keepdims=True)
    y = (xf - mu) * lax.rsqrt(var + LN_EPS)
    if g is not None:
        y = y * g.astype(F32) + b.astype(F32)
    return y.astype(x.dtype)

def _modulate(x, shift, scale):
    return _layer_norm(x) * (1.0 + scale) + shift

def _post_norm(x, y, g, b):
    return _layer_norm(DN_ALPHA * x + y, g, b)

def _swiglu(h, p):
    return (jax.nn.silu(h @ p['w_ffn_gate']) * (h @ p['w_ffn_up'])) @ p['w_ffn_down']

def _project(h, p):
    B, T, _ = h.shape
    offs = np.cumsum(SPLIT_SIZES)[:-1].tolist()
    (a, qm, km, vm, om, ig, fg, qa, ka, va, gates) = jnp.split(h @ p['w_in'], offs, axis=-1)

    def heads(t):
        return t.reshape(B, T, M_HEADS, M_HDIM).transpose(0, 2, 1, 3).astype(F32)

    m_i = (ig.reshape(B, T, 2, M_HEADS).astype(F32) + p['m_b_i']).transpose(2, 0, 3, 1)
    m_f = jax.nn.log_sigmoid(fg.reshape(B, T, 2, M_HEADS).astype(F32) + p['m_b_f']).transpose(2, 0, 3, 1)
    return {
        'pool': a,
        'm_q': heads(qm), 'm_k': heads(km) * (M_HDIM ** -0.5), 'm_v': heads(vm), 'm_o': om,
        'm_i': m_i, 'm_f': m_f,
        'a_q': qa.reshape(B, T, A_Q_HEADS, A_HDIM),
        'a_k': ka.reshape(B, T, A_KV_HEADS, A_HDIM),
        'a_v': va.reshape(B, T, A_KV_HEADS, A_HDIM),
        'gates': gates,
    }

def _pool_mixer(a, pool_w, pool_scale):
    B, T, _ = a.shape
    af = a.astype(F32)
    csum = jnp.concatenate([jnp.zeros((B, 1, POOL_WIDTH), F32), jnp.cumsum(af, axis=1)], axis=1)
    t = jnp.arange(T)
    outs = []
    for g, w in enumerate(POOL_WINDOWS):
        lo = jnp.clip(t - w // 2, 0, T)
        hi = jnp.clip(t - w // 2 + w, 0, T)
        sl = slice(g * POOL_GDIM, (g + 1) * POOL_GDIM)
        mean = (csum[:, hi, sl] - csum[:, lo, sl]) / (hi - lo).astype(F32)[None, :, None]
        outs.append(mean - af[:, :, sl])
    u = jnp.stack(outs, axis=2).astype(a.dtype)
    u = jnp.einsum('btgc,gcd->btgd', u, pool_w).reshape(B, T, POOL_WIDTH)
    return u * pool_scale

def _mlstm_chunk_step(state, xs):
    C, n, m = state
    q, k, v, ig, lf = xs
    L = q.shape[2]
    b = jnp.cumsum(lf, axis=-1)
    causal = jnp.tril(jnp.ones((L, L), bool))
    log_d = jnp.where(causal, b[..., :, None] - b[..., None, :] + ig[..., None, :], -jnp.inf)
    inter = b + m[..., None]
    m_row = jnp.maximum(inter, jnp.max(log_d, axis=-1))
    s = jnp.einsum('bhjd,bhtd->bhjt', q, k) * jnp.exp(log_d - m_row[..., None])
    w_inter = jnp.exp(inter - m_row)
    num = jnp.einsum('bhjt,bhtv->bhjv', s, v) + w_inter[..., None] * jnp.einsum('bhjd,bhdv->bhjv', q, C)
    nq = jnp.sum(s, axis=-1) + w_inter * jnp.einsum('bhjd,bhd->bhj', q, n)
    den = jnp.maximum(jnp.abs(nq), jnp.exp(-m_row))
    h = num / den[..., None]
    b_last = b[..., -1]
    g = b_last[..., None] - b + ig
    m_new = jnp.maximum(b_last + m, jnp.max(g, axis=-1))
    wk = jnp.exp(g - m_new[..., None])
    decay = jnp.exp(b_last + m - m_new)
    C_new = decay[..., None, None] * C + jnp.einsum('bht,bhtd,bhtv->bhdv', wk, k, v)
    n_new = decay[..., None] * n + jnp.einsum('bht,bhtd->bhd', wk, k)
    return (C_new, n_new, m_new), h

def _mlstm_scan(q, k, v, ig, lf, state):
    B, H, T, d = q.shape
    nc = T // M_CHUNK

    def chunks(a):
        return jnp.moveaxis(a.reshape(a.shape[:2] + (nc, M_CHUNK) + a.shape[3:]), 2, 0)

    state, h = lax.scan(_mlstm_chunk_step, state, (chunks(q), chunks(k), chunks(v), chunks(ig), chunks(lf)))
    return jnp.moveaxis(h, 0, 2).reshape(B, H, T, d), state

def _direction_inputs(pt, direction):
    parts = (pt['m_q'], pt['m_k'], pt['m_v'], pt['m_i'][direction], pt['m_f'][direction])
    if direction == 1:
        return tuple(jnp.flip(a, axis=2) for a in parts)
    return parts

def _mlstm_bidirectional(pl, pc):
    B = pl['m_q'].shape[0]
    zero = (jnp.zeros((B, M_HEADS, M_HDIM, M_HDIM), F32), jnp.zeros((B, M_HEADS, M_HDIM), F32),
            jnp.zeros((B, M_HEADS), F32))
    h_lat, h_ctx = None, None
    for direction in range(2):
        hc, state = _mlstm_scan(*_direction_inputs(pc, direction), zero)
        hl, _ = _mlstm_scan(*_direction_inputs(pl, direction), state)
        if direction == 1:
            hc, hl = jnp.flip(hc, axis=2), jnp.flip(hl, axis=2)
        h_lat = hl if h_lat is None else h_lat + hl
        h_ctx = hc if h_ctx is None else h_ctx + hc
    return h_lat, h_ctx

def _mlstm_readout(h, o, norm_w):
    B, H, T, d = h.shape
    mu = jnp.mean(h, -1, keepdims=True)
    var = jnp.mean(jnp.square(h - mu), -1, keepdims=True)
    hn = ((h - mu) * lax.rsqrt(var + LN_EPS)).transpose(0, 2, 1, 3).reshape(B, T, M_WIDTH)
    return (hn * norm_w.astype(F32) * jax.nn.sigmoid(o.astype(F32))).astype(o.dtype)

def _axial_rope_tables(n_tokens):
    rows = n_tokens // GRID_W
    row = jnp.repeat(jnp.arange(rows, dtype=F32), GRID_W)
    col = jnp.tile(jnp.arange(GRID_W, dtype=F32), rows)
    inv = ROPE_BASE ** (-jnp.arange(ROPE_PAIRS, dtype=F32) / ROPE_PAIRS)
    ang = jnp.concatenate([row[:, None] * inv, col[:, None] * inv], axis=-1)
    return jnp.cos(ang), jnp.sin(ang)

def _apply_axial_rope(x, cos, sin):
    B, T, H, d = x.shape
    xr = x.astype(F32).reshape(B, T, H, 2, 2, ROPE_PAIRS)
    x1, x2 = xr[..., 0, :], xr[..., 1, :]
    c = cos.reshape(T, 1, 2, ROPE_PAIRS)
    s = sin.reshape(T, 1, 2, ROPE_PAIRS)
    out = jnp.stack([x1 * c - x2 * s, x2 * c + x1 * s], axis=-2)
    return out.reshape(B, T, H, d).astype(x.dtype)

def _sink_attend(q, ks, vs, masks, sink):
    scale = A_HDIM ** -0.5
    logits = []
    for k, msk in zip(ks, masks):
        s = jnp.einsum('bqhgd,bkhd->bhgqk', q, k).astype(F32) * scale
        if msk is not None:
            s = jnp.where(msk, s, -jnp.inf)
        logits.append(s)
    B, Q = q.shape[:2]
    logits.append(jnp.broadcast_to(sink.astype(F32)[None, :, :, None, None], (B,) + sink.shape + (Q, 1)))
    p = jax.nn.softmax(jnp.concatenate(logits, axis=-1), axis=-1)
    out, off = None, 0
    for v, s in zip(vs, logits[:-1]):
        nk = s.shape[-1]
        o = jnp.einsum('bhgqk,bkhd->bqhgd', p[..., off:off + nk].astype(v.dtype), v)
        out = o if out is None else out + o
        off += nk
    return out

def _windowed_attention(q, k, v, kc, vc, sink):
    B, T = q.shape[:2]
    nb = T // A_BLOCK
    band = 3 * A_BLOCK
    pad = ((0, 0), (A_BLOCK, A_BLOCK), (0, 0), (0, 0))
    kp, vp = jnp.pad(k, pad), jnp.pad(v, pad)

    def block(i):
        start = i * A_BLOCK
        qb = lax.dynamic_slice_in_dim(q, start, A_BLOCK, axis=1)
        kb = lax.dynamic_slice_in_dim(kp, start, band, axis=1)
        vb = lax.dynamic_slice_in_dim(vp, start, band, axis=1)
        qpos = start + jnp.arange(A_BLOCK)
        kpos = start - A_BLOCK + jnp.arange(band)
        valid = ((jnp.abs(qpos[:, None] - kpos[None, :]) <= WINDOW)
                 & (kpos >= 0)[None, :] & (kpos < T)[None, :])
        return _sink_attend(qb, (kb, kc), (vb, vc), (valid, None), sink)

    out = lax.map(block, jnp.arange(nb))
    return jnp.moveaxis(out, 0, 1).reshape(B, T, A_Q_WIDTH)

def _merge(gates, branch_outs, p):
    B, T, _ = gates.shape
    g = jax.nn.sigmoid(gates.astype(F32)).astype(gates.dtype).reshape(B, T, N_BRANCH, D_MODEL)
    y = None
    for i, u in enumerate(branch_outs):
        yi = g[:, :, i] * (u @ p['w_branch'][i])
        y = yi if y is None else y + yi
    return y @ p['w_out']

def _trunk_layer(x, ctx, mod_x, mod_c, p, cos, sin, last):
    sh1, sc1, g1, sh2, sc2, g2 = jnp.split(mod_x, 6, axis=-1)
    csh1, csc1, cg1, csh2, csc2, cg2 = jnp.split(mod_c, 6, axis=-1)
    B, T, _ = x.shape
    px = _project(_modulate(x, sh1, sc1), p)
    pc = _project(_modulate(ctx, csh1, csc1), p)
    pool_x = _pool_mixer(px['pool'], p['pool_w'], p['pool_scale'])
    h_lat, h_ctx = _mlstm_bidirectional(px, pc)
    mlstm_x = _mlstm_readout(h_lat, px['m_o'], p['m_norm_w'])
    qx = _apply_axial_rope(px['a_q'], cos, sin).reshape(B, T, A_KV_HEADS, A_GROUP, A_HDIM)
    kx = _apply_axial_rope(px['a_k'], cos, sin)
    attn_x = _windowed_attention(qx, kx, px['a_v'], pc['a_k'], pc['a_v'], p['attn_sink'])
    mix_x = _merge(px['gates'], (pool_x, mlstm_x, attn_x), p)
    x = _post_norm(x, g1 * mix_x, p['ln1_g'], p['ln1_b'])
    x = _post_norm(x, g2 * _swiglu(_modulate(x, sh2, sc2), p), p['ln2_g'], p['ln2_b'])
    if not last:
        Bc, Lc, _ = ctx.shape
        pool_c = _pool_mixer(pc['pool'], p['pool_w'], p['pool_scale'])
        mlstm_c = _mlstm_readout(h_ctx, pc['m_o'], p['m_norm_w'])
        qc = pc['a_q'].reshape(Bc, Lc, A_KV_HEADS, A_GROUP, A_HDIM)
        attn_c = _sink_attend(qc, (pc['a_k'],), (pc['a_v'],), (None,), p['attn_sink']).reshape(Bc, Lc, A_Q_WIDTH)
        mix_c = _merge(pc['gates'], (pool_c, mlstm_c, attn_c), p)
        ctx = _post_norm(ctx, cg1 * mix_c, p['ln1_g'], p['ln1_b'])
        ctx = _post_norm(ctx, cg2 * _swiglu(_modulate(ctx, csh2, csc2), p), p['ln2_g'], p['ln2_b'])
    return x, ctx

def setup_inputs(seed: int = 0) -> dict:
    key = jax.random.key(seed)
    ks = jax.random.split(key, 24)
    L = DEPTH

    def nrm(k, shape, s):
        return jax.random.normal(k, shape, F32) * s

    return {
        'x': nrm(ks[0], (BATCH, SEQ, D_MODEL), 1.0),
        'c': nrm(ks[1], (BATCH, D_MODEL), 1.0),
        'ctx': nrm(ks[2], (BATCH, CTX_LEN, D_MODEL), 1.0),
        'c_ctx': nrm(ks[3], (D_MODEL,), 1.0),
        'w_mod': nrm(ks[4], (L, D_MODEL, 6 * D_MODEL), 0.5 * D_MODEL ** -0.5),
        'b_mod': nrm(ks[5], (L, 6 * D_MODEL), 0.01),
        'w_in': nrm(ks[6], (L, D_MODEL, IN_WIDTH), D_MODEL ** -0.5),
        'pool_w': nrm(ks[7], (L, POOL_GROUPS, POOL_GDIM, POOL_GDIM), POOL_GDIM ** -0.5),
        'pool_scale': 1.0 + nrm(ks[8], (L, POOL_WIDTH), 0.02),
        'm_b_i': nrm(ks[9], (L, 2, M_HEADS), 0.1),
        'm_b_f': jnp.linspace(3.0, 6.0, M_HEADS, dtype=F32) + nrm(ks[10], (L, 2, M_HEADS), 0.1),
        'm_norm_w': 1.0 + nrm(ks[11], (L, M_WIDTH), 0.02),
        'attn_sink': nrm(ks[12], (L, A_KV_HEADS, A_GROUP), 0.5),
        'w_branch': nrm(ks[13], (L, N_BRANCH, BRANCH_WIDTH, D_MODEL), BRANCH_WIDTH ** -0.5),
        'w_out': nrm(ks[14], (L, D_MODEL, D_MODEL), DN_BETA * D_MODEL ** -0.5),
        'ln1_g': 1.0 + nrm(ks[15], (L, D_MODEL), 0.02),
        'ln1_b': nrm(ks[16], (L, D_MODEL), 0.02),
        'ln2_g': 1.0 + nrm(ks[17], (L, D_MODEL), 0.02),
        'ln2_b': nrm(ks[18], (L, D_MODEL), 0.02),
        'w_ffn_gate': nrm(ks[19], (L, D_MODEL, D_FF), D_MODEL ** -0.5),
        'w_ffn_up': nrm(ks[20], (L, D_MODEL, D_FF), D_MODEL ** -0.5),
        'w_ffn_down': nrm(ks[21], (L, D_FF, D_MODEL), DN_BETA * D_FF ** -0.5),
    }

def reference(x, c, ctx, c_ctx, w_mod, b_mod, w_in, pool_w, pool_scale, m_b_i, m_b_f, m_norm_w,
              attn_sink, w_branch, w_out, ln1_g, ln1_b, ln2_g, ln2_b, w_ffn_gate, w_ffn_up, w_ffn_down):
    cos, sin = _axial_rope_tables(x.shape[1])
    silu_c = jax.nn.silu(c)
    silu_cc = jax.nn.silu(c_ctx)
    for l in range(DEPTH):
        p = {
            'w_in': w_in[l], 'pool_w': pool_w[l], 'pool_scale': pool_scale[l],
            'm_b_i': m_b_i[l], 'm_b_f': m_b_f[l], 'm_norm_w': m_norm_w[l], 'attn_sink': attn_sink[l],
            'w_branch': w_branch[l], 'w_out': w_out[l],
            'ln1_g': ln1_g[l], 'ln1_b': ln1_b[l], 'ln2_g': ln2_g[l], 'ln2_b': ln2_b[l],
            'w_ffn_gate': w_ffn_gate[l], 'w_ffn_up': w_ffn_up[l], 'w_ffn_down': w_ffn_down[l],
        }
        mod_x = (silu_c @ w_mod[l] + b_mod[l])[:, None, :]
        mod_c = silu_cc @ w_mod[l] + b_mod[l]
        x, ctx = _trunk_layer(x, ctx, mod_x, mod_c, p, cos, sin, l == DEPTH - 1)
    return x


_drawn_inputs = setup_inputs


def setup_inputs(seed=0):
    import zlib

    import numpy as np

    out = dict(_drawn_inputs(seed))
    spreads = {}
    factors = {'ctx': 3.78,
     'c_ctx': 3.193,
     'b_mod': 8.0,
     'pool_scale': 37.85,
     'm_b_i': 25.349,
     'm_norm_w': 60.675,
     'attn_sink': 64.0}
    for name, (base, spread) in spreads.items():
        noise = np.random.default_rng([zlib.crc32(name.encode()), seed]).standard_normal(out[name].shape)
        drawn = base * np.exp(spread * noise) if base else spread * noise
        out[name] = __import__('jax').numpy.asarray(drawn.astype(out[name].dtype))
    for name, factor in factors.items():
        out[name] = (out[name] * factor).astype(out[name].dtype)
    return out
```

```python
from contextlib import ExitStack

import numpy as np

import concourse.bass as bass
from concourse import mybir

ALU = mybir.AluOpType
ACT = mybir.ActivationFunctionType
F32 = mybir.dt.float32
F32R = mybir.dt.float32r
BF16 = mybir.dt.bfloat16
AX_X = mybir.AxisListType.X

P = 128
D = 1024
SEQ = 512
CTX = 256
TOK = SEQ + CTX
DEPTH = 2
KB = D // P
NT = TOK // P
LT = SEQ // P
BW = D // 2
UB = BW // P
HEADS = 4
HD = 128
AH = 64
PAIRS = 4
FF = 2816
FB = FF // P
FG = [8, 8, 6]
MB = 6 * KB
SHIFT1, SCALE1, GATE1, SHIFT2, SCALE2, GATE2 = (KB * i for i in range(6))
ALPHA = (2 * DEPTH) ** 0.25
EPS = 1e-5
MASKED = -1e30
PAD = 8
LAT0 = PAD
CTX0 = LAT0 + SEQ + 2 * PAD
PW = CTX0 + CTX + PAD
LATW = LAT0 + SEQ + PAD
SBUF_START, SBUF_END = 16512, 229344
WINDOWS = (2, 4, 8, 16)
MODS_FIRST = 20
IN_TILES = 28
LAYER_TILES = IN_TILES + 48 + KB + sum(2 * g + KB for g in FG)
BLOCKS = 9 + 2 + PAIRS + 4 * HEADS + 6 * KB + KB + sum(2 * g + KB for g in FG)
CONST_ALL = 16 * 8
ROWS = 36
ALL = ((0, SEQ), (SEQ, CTX))
LATENT = ((0, SEQ),)


class Count:

    def __init__(self):
        self.n, self.reg, self.step = {}, None, {}

    def next(self, sem, k=1):
        self.n[sem.name] = self.n.get(sem.name, 0) + k
        return self.now(sem)

    def now(self, sem, back=0):
        v = self.n.get(sem.name, 0) - back
        s = self.step.get(sem.name, 0)
        return self.reg * s + v if self.reg is not None and s else v

    def sig(self, sem, k=1):
        self.n[sem.name] = self.n.get(sem.name, 0) + k
        return k

    def enter(self, reg, step):
        self.reg, self.step = reg, {s.name: k for s, k in step.items()}
        self.at = dict(self.n)

    def leave(self, times):
        for name, v in self.n.items():
            per = v - self.at.get(name, 0)
            assert per == self.step.get(name, 0), (name, per, self.step.get(name, 0))
            self.n[name] = self.at.get(name, 0) + per * times
        self.reg, self.step = None, {}


def trunk(nc, x_lat, ctx, cvec, w_mod, b_mod, w_tiles, vecs, ifbias, sinks, ln_gb, consts, tables, pool_inv, out):
    with ExitStack() as stack:
        def sem(name):
            return stack.enter_context(nc.semaphore(name))

        cursor = [SBUF_START]

        def place(name, shape, dt=F32, at=None):
            size = (int(np.prod(shape[1:])) * (2 if dt == BF16 else 4) + 31) // 32 * 32
            spot = cursor if at is None else at
            t = nc.alloc_sbuf_tensor_at(name, list(shape), dt, offset=spot[0])
            spot[0] += size
            assert spot[0] <= (SBUF_END if at is None else at[1]), (name, spot)
            return t

        def region(size):
            start = cursor[0]
            cursor[0] += size
            return start, start + size

        raw = [place(f"raw{i}", [P, KB, P]) for i in range(2)]
        w_hi = [place(f"w_hi{i}", [P, KB, P], F32R) for i in range(2)]
        w_lo = [place(f"w_lo{i}", [P, KB, P], F32R) for i in range(2)]
        mod_raw = [place(f"mod_raw{i}", [P, KB, P]) for i in range(2)]
        h_hi = place("h_hi", [P, KB, TOK], F32R)
        h_lo = place("h_lo", [P, KB, TOK], F32R)
        ident = place("ident", [P, P])
        rot = place("rot", [P, P])
        ident16 = place("ident16", [P, P], BF16)
        mask16 = place("mask16", [P, 2, P], BF16)
        modv = [place(f"modv{i}", [P, MB, 2]) for i in range(DEPTH)]
        bmod = place("bmod", [P, DEPTH, MB])
        vec = place("vec", [P, DEPTH, 2, UB])
        ifb = place("ifb", [ROWS, DEPTH, 2])
        sink = place("sink", [P, DEPTH, 8])
        negsink = place("negsink", [P, DEPTH, 8])
        cin = place("cin", [P, KB, 2])
        cact = place("cact", [P, KB, 2])
        stats = place("stats", [P, NT, 2, 6])
        aggr = place("aggr", [P, NT, 2])
        rstd = place("rstd", [P, NT])
        nmr = place("nmr", [P, NT])
        root = place("root", [P, NT])
        eps = place("eps", [P, 1])
        u_region = region(3 * 2 * UB * TOK * 4)
        x_region = region(NT * D * 4)
        t_region = (cursor[0], SBUF_END)

        def sub(r, start, size=None):
            return [r[0] + start, r[0] + start + size if size else r[1]]

        r = sub(u_region, 0)
        u_hi = [place(f"u_hi{i}", [P, UB, TOK], F32R, at=r) for i in range(3)]
        u_lo = [place(f"u_lo{i}", [P, UB, TOK], F32R, at=r) for i in range(3)]
        r = sub(u_region, 0)
        f_hi = place("f_hi", [P, 8, TOK], F32R, at=r)
        f_lo = place("f_lo", [P, 8, TOK], F32R, at=r)
        r = sub(u_region, 0)
        xn = place("xn", [P, NT, D], at=r)
        mod32 = [place(f"mod32_{i}", [P, 4, P], at=r) for i in range(2)]
        ln_g = place("ln_g", [P, D], at=r)
        ln_b = place("ln_b", [P, D], at=r)
        mask32 = place("mask32", [P, 2, P], at=sub(t_region, 0))
        res = place("res", [P, NT, D], at=sub(x_region, 0))
        y32 = place("y32", [P, KB, TOK], at=sub(x_region, 0))
        r = sub(t_region, 0)
        gated = [place(f"gated{i}", [P, TOK], at=r) for i in range(2)]
        value = [place(f"value{i}", [P, TOK], at=r) for i in range(2)]
        prod = place("prod", [P, TOK], at=r)
        y_out = [place(f"y_out{i}", [P, TOK], at=r) for i in range(2)]
        r = sub(x_region, 0)
        apad = [place(f"apad{i}", [P, PW], at=r) for i in range(2)]
        sums = [place(f"sums{i}", [P, PW], at=r) for i in range(2)]
        inv = [place(f"inv{i}", [P, PW], at=r) for i in range(2)]
        pool_u = place("pool_u", [P, TOK], at=r)
        r = sub(t_region, 0)
        pu_hi = [place(f"pu_hi{i}", [P, TOK], F32R, at=r) for i in range(2)]
        pu_lo = [place(f"pu_lo{i}", [P, TOK], F32R, at=r) for i in range(2)]
        pool_y = [place(f"pool_y{i}", [P, TOK], at=r) for i in range(2)]
        ig = place("ig", [ROWS, TOK], at=r)
        fg = place("fg", [ROWS, TOK], at=r)
        r = sub(x_region, 0)
        cos = place("cos", [P, SEQ], at=r)
        sin = place("sin", [P, SEQ], at=r)
        kT = place("kT", [P, TOK], at=r)
        qT = place("qT", [P, TOK], at=r)
        vT = place("vT", [P, TOK], at=r)
        vaug = place("vaug", [P, NT, 2, AH + 1], at=r)
        rope_c = place("rope_c", [P, SEQ], at=r)
        rope_s = place("rope_s", [P, SEQ], at=r)
        r = sub(t_region, 0)
        probs = [place(f"probs{i}", [P, 5, P], at=r) for i in range(2)]
        probsT = [place(f"probsT{i}", [P, 5, P], at=r) for i in range(2)]
        att = place("att", [P, NT, P], at=r)
        mx = place("mx", [P, 2, 2], at=r)
        mrow = place("mrow", [P, 2], at=r)
        negm = place("negm", [P, 2], at=r)
        esink = place("esink", [P, 2], at=r)
        den = place("den", [P, 2], at=r)
        rden = place("rden", [P, 2], at=r)
        r = sub(x_region, 0)
        r_i = place("r_i", [ROWS, TOK], at=r)
        r_a = place("r_a", [ROWS, TOK], at=r)
        r_b = place("r_b", [ROWS, TOK], at=r)
        r_m = place("r_m", [ROWS, TOK], at=r)
        r_t = place("r_t", [ROWS, TOK], at=r)
        r_w = place("r_w", [ROWS, TOK], at=r)
        zeros = place("zeros", [ROWS, P], at=r)
        m_in = place("m_in", [ROWS, NT + 1], at=r)
        r_dec = place("r_dec", [ROWS, NT], at=r)
        r_e = place("r_e", [ROWS, TOK], at=sub(u_region, UB * TOK * 4))
        n_row = [place(f"n_row{i}", [ROWS, TOK], at=sub(u_region, (4 * UB + i) * TOK * 4)) for i in range(4)]
        r = sub(t_region, 0)
        neg_m = place("neg_m", [ROWS, TOK], at=r)
        cols = place("cols", [P, NT, 4, ROWS], at=r)
        decay = place("decay", [P, 2 * HEADS, NT], at=r)
        hwork = place("hwork", [P, NT, HD], at=r)
        hstat = place("hstat", [P, NT, 6], at=r)
        haggr = place("haggr", [P, NT, 2], at=r)
        hrstd = place("hrstd", [P, NT], at=r)
        hroot = place("hroot", [P, NT], at=r)
        denr = place("denr", [P, NT, 2], at=r)
        rdenr = place("rdenr", [P, NT, 2], at=r)
        total = place("total", [P, NT, 2, HD + 1], at=r)
        state = place("state", [P, NT, 2, HD + 1], at=r)
        inter = place("inter", [P, 2, HD + 1], at=r)
        r = sub(x_region, 0)
        hq = place("hq", [P, TOK], at=r)
        hk = place("hk", [P, TOK], at=r)
        hv = place("hv", [P, TOK], at=r)
        ho = place("ho", [P, TOK], at=r)
        k_tok = place("k_tok", [P, NT, P], at=r)
        v_tok = place("v_tok", [P, NT, HD + 1], at=r)
        vw = [place(f"vw{i}", [P, HD + 1], at=r) for i in range(2)]
        wexp = [place(f"wexp{i}", [P, 2, P], at=r) for i in range(2)]

        ps = stack.enter_context(nc.psum_tensor("ps", [P, 8, 512], F32))
        spill = nc.dram_tensor("res_spill", [TOK, D], F32, kind="Internal").ap()

        raw_full = [sem("raw_full0"), sem("raw_full1")]
        mod_full = [sem("mod_full0"), sem("mod_full1")]
        hi_done, lo_done = sem("hi_done"), sem("lo_done")
        mod_done = sem("mod_done")
        blk_done, blk_out = sem("blk_done"), sem("blk_out")
        phase = sem("phase")
        const_in, tab_in = sem("const_in"), sem("tab_in")
        inv_in = [sem("inv_in0"), sem("inv_in1")]
        x_in = [sem(f"x_in{i}") for i in range(NT)]
        stored = sem("stored")
        a_step, v_step = sem("a_step"), sem("v_step")
        mod_ready = sem("mod_ready")
        var_done, root_done = sem("var_done"), sem("root_done")
        stat_done, normed = sem("stat_done"), sem("normed")
        x_new = sem("x_new")
        xt_done, xt_act = sem("xt_done"), sem("xt_act")
        h_ready = sem("h_ready")
        pu_ready, pu_used, py_free = sem("pu_ready"), sem("pu_used"), sem("py_free")
        rot_done, rope_done = sem("rot_done"), sem("rope_done")
        vt_done, vt_evac = sem("vt_done"), sem("vt_evac")
        s_done, s_max, p_exp, pt_done, pt_evac, pv_done, pv_evac = (
            sem(n) for n in ("s_done", "s_max", "p_exp", "pt_done", "pt_evac", "pv_done", "pv_evac"))
        at_done, at_evac = sem("at_done"), sem("at_evac")
        row_act, row_dve, row_pe, row_evac = (sem(n) for n in ("row_act", "row_dve", "row_pe", "row_evac"))
        kt_done, kt_evac, v_evac = sem("kt_done"), sem("kt_evac"), sem("v_evac")
        vw_done, st_done, st_step = sem("vw_done"), sem("st_done"), sem("st_step")
        e_done, e_exp, w_done, n_done, i_evac, n_add = (
            sem(n) for n in ("e_done", "e_exp", "w_done", "n_done", "i_evac", "n_add"))
        hr_ready, hr_done, hr_evac = sem("hr_ready"), sem("hr_done"), sem("hr_evac")
        pair_free = sem("pair_free")
        room = sem("room")
        y_split = sem("y_split")
        tr_done, tr_free = sem("tr_done"), sem("tr_free")

        block = stack.enter_context(nc.Block())

        def live(l):
            return LATENT if l == DEPTH - 1 else ALL

        def tiles_of(l):
            return LT if l == DEPTH - 1 else NT

        def over(eng, c):
            eng.drain().then_inc(phase, 1)
            eng.wait_ge(phase, c.next(phase, 3))

        def scan_index(direction, chunk):
            if direction == 0:
                return (NT - LT) + chunk if chunk < LT else chunk - LT
            return NT - 1 - chunk

        def chunk_at(direction, s):
            return next(k for k in range(NT) if scan_index(direction, k) == s)

        def units(l):
            return [(i, x) for i in range(tiles_of(l)) for x in range(2)]

        def band(i):
            return [j for j in (i - 1, i, i + 1) if 0 <= j < LT] if i < LT else []

        def keys(i):
            b = band(i)
            return [(j, n) for n, j in enumerate(b + list(range(LT, NT)))]

        STATES = [(s, d) for s in range(NT - 1) for d in range(2)]

        @block.sync
        def _(sp):
            c = Count()

            def load_pair(n, blocks, first=False):
                for j in range(2):
                    if not first:
                        sp.wait_ge(lo_done, c.next(lo_done))
                    width = blocks[j] * P
                    sp.dma_start(raw[j][:].rearrange("p k m -> p (k m)")[:, 0:width],
                                 w_tiles[n + j, :, 0:width]).then_inc(raw_full[j], 16)

            def load_mods(m, first=False):
                for j in range(2):
                    if not first:
                        sp.wait_ge(mod_done, c.next(mod_done))
                    sp.dma_start(mod_raw[j][:].rearrange("p k m -> p (k m)"), w_mod[m + j]).then_inc(mod_full[j], 16)

            def run(n, pairs, blocks, m=None, every=1):
                step = {lo_done: 2 * every}
                if m is not None:
                    step[mod_done] = 2
                with sp.Fori(0, pairs // every) as i:
                    c.enter(i, step)
                    for k in range(every):
                        load_pair(n + 2 * every * i + 2 * k, blocks)
                        if m is not None and k == 0:
                            load_mods(m + 2 * i)
                    c.leave(pairs // every)
                return n + 2 * pairs

            load_mods(0, first=True)
            load_pair(0, (KB, KB), first=True)
            for m in range(2, MODS_FIRST, 2):
                load_mods(m)
            m = MODS_FIRST
            load_mods(m)
            load_pair(2, (KB, KB))
            load_mods(m + 2)
            m += 4
            n = run(4, (IN_TILES - 4) // 2, (KB, KB))
            n = run(n, 3 * KB, (KB, UB), m, every=2)
            m += 3 * KB
            n = run(n, MB // 2, (KB, KB), m)
            for l in range(DEPTH):
                if l:
                    n = run(n, IN_TILES // 2, (KB, KB))
                    n = run(n, 3 * KB, (KB, UB))
                last = (l + 1) * LAYER_TILES - KB
                n = run(n, (last - n) // 2, (KB, KB))
                n = run(n, KB // 2, (FG[-1], FG[-1]))

        @block.gpsimd
        def _(pool):
            c = Count()
            with pool.Fori(0, DEPTH * LAYER_TILES // 2) as i:
                c.enter(i, {hi_done: 2, lo_done: 2})
                for j in range(2):
                    pool.wait_ge(hi_done, c.next(hi_done))
                    nc.gpsimd.tensor_tensor(w_lo[j][:], raw[j][:], w_hi[j][:].bitcast(F32),
                                            ALU.subtract).then_inc(lo_done, c.sig(lo_done))
                c.leave(DEPTH * LAYER_TILES // 2)

        @block.tensor
        def _(pe):
            c = Count()

            def product(slot, buf, k_blocks, rhs, chunks, w0=0, fresh=True, spare=1):
                if fresh:
                    pe.wait_ge(lo_done, c.next(lo_done))
                free = c.now(blk_done, spare)
                if not isinstance(free, int) or free > 0:
                    pe.wait_ge(blk_out, free)
                a_hi, a_lo = rhs
                for k in range(k_blocks):
                    for p, (w, a) in enumerate(((w_hi, a_hi), (w_hi, a_lo), (w_lo, a_hi))):
                        for q, (t0, size) in enumerate(chunks):
                            mm = nc.tensor.matmul(ps[:, 2 * buf + q, 0:size], w[slot][:, w0 + k, :],
                                                  a[:, k, t0:t0 + size], start=(k == 0 and p == 0),
                                                  stop=(k == k_blocks - 1 and p == 2))
                mm.then_inc(blk_done, c.sig(blk_done))

            def modulation(slot, out_ap):
                pe.wait_ge(mod_full[slot], c.next(mod_full[slot], 16))
                for k in range(KB):
                    mm = nc.tensor.matmul(out_ap, mod_raw[slot][:, k, :], cact[:, k, :],
                                          start=(k == 0), stop=(k == KB - 1))
                mm.then_inc(mod_done, c.sig(mod_done))

            def mod_beside(slot, buf, spare=1):
                free = c.now(blk_done, spare)
                if not isinstance(free, int) or free > 0:
                    pe.wait_ge(blk_out, free)
                modulation(slot, ps[:, 2 * buf + 1, 508:510])

            def norm_turns(l, after_post=True):
                if after_post:
                    c.next(normed, tiles_of(l))
                for t in range(tiles_of(l)):
                    pe.wait_ge(normed, c.next(normed))
                    for half in range(2):
                        if c.now(xt_done) >= 2:
                            pe.wait_ge(xt_act, c.now(xt_done, 1))
                        for k in range(4):
                            mm = nc.tensor.transpose(ps[:, 4 + half, k * P:(k + 1) * P],
                                                     xn[:, t, (4 * half + k) * P:(4 * half + k + 1) * P], ident[:])
                        mm.then_inc(xt_done, c.sig(xt_done))

            def turn_back(par, chunks):
                pe.wait_ge(tr_free, c.now(tr_done, -1))
                for q, (t0, size) in enumerate(chunks):
                    for t in range(size // P):
                        mm = nc.tensor.transpose(ps[:, 4 + 2 * par + q, t * P:(t + 1) * P],
                                                 y_out[par][:, t0 + t * P:t0 + (t + 1) * P], ident[:])
                mm.then_inc(tr_done, c.sig(tr_done))

            pe.wait_ge(const_in, CONST_ALL)
            pe.wait_ge(a_step, 1)
            c.next(a_step)
            for m in range(MODS_FIRST):
                modulation(m % 2, ps[:, 6, 2 * m:2 * m + 2])
            norm_turns(0, after_post=False)
            over(pe, c)
            for l in range(DEPTH):
                chunks = live(l)
                lt = tiles_of(l)
                b0 = c.now(blk_done)
                for g in range(UB):
                    if l == 0:
                        mod_beside(g % 2, (b0 + g) % 2)
                    product(g % 2, (b0 + g) % 2, KB, (h_hi, h_lo), chunks)
                product(0, (b0 + UB) % 2, KB, (h_hi, h_lo), ALL)
                for g in range(UB):
                    pe.wait_ge(pu_ready, c.next(pu_ready))
                    product(1, (b0 + UB + 1 + g) % 2, 1, (pu_hi[g % 2][:].unsqueeze(1), pu_lo[g % 2][:].unsqueeze(1)),
                            chunks, w0=g, fresh=(g == 0))
                over(pe, c)

                product(0, 0, KB, (h_hi, h_lo), ALL, spare=0)
                product(1, 0, KB, (h_hi, h_lo), ALL, spare=0)

                def rotate(z):
                    nc.tensor.matmul(ps[:, 3, 0:SEQ], rot[:], z[:, 0:SEQ], start=True,
                                     stop=True).then_inc(rot_done, c.sig(rot_done))

                pe.wait_ge(blk_out, c.now(blk_done))
                rotate(kT)
                for t in range(NT):
                    mm = nc.tensor.transpose(ps[:, 6 + t // 4, (t % 4) * P:(t % 4 + 1) * P],
                                             vT[:, t * P:(t + 1) * P], ident[:])
                mm.then_inc(vt_done, c.sig(vt_done))
                pe.wait_ge(vt_evac, c.next(vt_evac))
                pe.wait_ge(rope_done, c.next(rope_done))
                for p in range(PAIRS):
                    product(p % 2, 0, KB, (h_hi, h_lo), chunks, spare=0)
                    pe.wait_ge(blk_out, c.now(blk_done))
                    rotate(qT)
                    pe.wait_ge(rope_done, c.next(rope_done))
                    U = units(l)
                    first = c.now(s_done)

                    def scores(n):
                        i, x = U[n]
                        rows = slice(AH * x, AH * x + AH)
                        if first + n:
                            pe.wait_ge(p_exp, first + n)
                        q = qT[rows, i * P:(i + 1) * P]
                        b = band(i)
                        if b:
                            width = len(b) * P
                            edge = [(n_, mask16[:, 0 if j < i else 1, :]) for n_, j in enumerate(b) if j != i]
                            nc.tensor.matmul(ps[:, 4, 0:width], q, kT[rows, b[0] * P:(b[-1] + 1) * P],
                                             start=True, stop=not edge)
                            for e, (n_, mask) in enumerate(edge):
                                nc.tensor.matmul(ps[:, 4, n_ * P:(n_ + 1) * P], ident16[:], mask,
                                                 start=False, stop=e == len(edge) - 1)
                        nc.tensor.matmul(ps[:, 5, 0:CTX], q, kT[rows, SEQ:TOK], start=True,
                                         stop=True).then_inc(s_done, c.sig(s_done))

                    scores(0)
                    for n, (i, x) in enumerate(U):
                        if n + 1 < len(U):
                            scores(n + 1)
                        pe.wait_ge(p_exp, first + n + 1)
                        if first + n:
                            pe.wait_ge(pt_evac, first + n)
                        for j, place_ in keys(i):
                            mm = nc.tensor.transpose(ps[:, 6 + place_ // 4, (place_ % 4) * P:(place_ % 4 + 1) * P],
                                                     probs[n % 2][:, place_, :], ident[:])
                        mm.then_inc(pt_done, c.sig(pt_done))
                        pe.wait_ge(pt_evac, first + n + 1)
                        if first + n:
                            pe.wait_ge(pv_evac, first + n)
                        for m_, (j, place_) in enumerate(keys(i)):
                            mm = nc.tensor.matmul(ps[:, 2, 0:AH + 1], probsT[n % 2][:, place_, :], vaug[:, j, x, :],
                                                  start=(m_ == 0), stop=(m_ == len(keys(i)) - 1))
                        mm.then_inc(pv_done, c.sig(pv_done))
                    pe.wait_ge(pv_evac, first + len(U))
                    for t in range(lt):
                        mm = nc.tensor.transpose(ps[:, 6 + t // 4, (t % 4) * P:(t % 4 + 1) * P], att[:, t, :], ident[:])
                    mm.then_inc(at_done, c.sig(at_done))
                    pe.wait_ge(at_evac, c.next(at_evac))
                over(pe, c)

                pe.wait_ge(row_dve, c.next(row_dve, 2))
                for t in range(NT):
                    for q in range(4):
                        at_ = ((t % 3) * 4 + q) * ROWS
                        nc.tensor.transpose(ps[:, 4 + t // 3, at_:at_ + ROWS], n_row[q][:, t * P:(t + 1) * P],
                                            ident[0:ROWS, 0:ROWS])
                for d in range(2):
                    for hd in range(HEADS):
                        row, at_ = 32 * d + hd, (HEADS * d + hd) * NT
                        mm = nc.tensor.matmul(ps[:, 6, at_:at_ + NT], ident[0:ROWS, row:row + 1].broadcast_to([ROWS, P]),
                                              r_dec[:], start=True, stop=True)
                mm.then_inc(row_pe, c.sig(row_pe))
                pe.wait_ge(row_evac, c.next(row_evac))
                for hd in range(HEADS):
                    b = c.now(blk_done)
                    for j, ch in enumerate((chunks, ALL, ALL, chunks)):
                        product(j % 2, (b + j) % 2, KB, (h_hi, h_lo), ch, spare=1 if j or hd else 0)
                    pe.wait_ge(blk_out, b + 3)
                    for src, bank in ((hk, 6), (hv, 4)):
                        for t in range(NT):
                            mm = nc.tensor.transpose(ps[:, bank + t // 4, (t % 4) * P:(t % 4 + 1) * P],
                                                     src[:, t * P:(t + 1) * P], ident[:])
                        mm.then_inc(kt_done, c.sig(kt_done))
                    pe.wait_ge(kt_evac, c.next(kt_evac))
                    pe.wait_ge(v_evac, c.next(v_evac))
                    for s, d in STATES:
                        pe.wait_ge(vw_done, c.next(vw_done))
                        if c.now(st_done) >= 2:
                            pe.wait_ge(st_step, c.now(st_done, 1))
                        nc.tensor.matmul(ps[:, 6 + d, 0:HD + 1], k_tok[:, chunk_at(d, s), :], vw[d][:],
                                         start=True, stop=True).then_inc(st_done, c.sig(st_done))
                    pe.wait_ge(st_step, c.now(st_done))
                    first = c.now(e_done)

                    def weights_of(t):
                        if first + t >= 2:
                            pe.wait_ge(w_done, first + t - 1)
                        if first + t:
                            pe.wait_ge(i_evac, first + t)
                        bank = 4 + t % 2
                        nc.tensor.matmul(ps[:, bank, 0:2 * P], ident16[:], mask16[:].rearrange("p a b -> p (a b)"),
                                         start=True, stop=False)
                        for d in range(2):
                            row = 32 * d + hd
                            nc.tensor.matmul(ps[:, bank, d * P:(d + 1) * P],
                                             ident[0:ROWS, row:row + 1].broadcast_to([ROWS, P]),
                                             neg_m[:, t * P:(t + 1) * P], start=False, stop=d == 1)
                        nc.tensor.matmul(ps[:, bank, 2 * P:3 * P], hk[:, t * P:(t + 1) * P], hq[:, t * P:(t + 1) * P],
                                         start=True, stop=True)
                        for d in range(2):
                            mm = nc.tensor.matmul(ps[:, 7, d * (HD + 1):(d + 1) * (HD + 1)], hq[:, t * P:(t + 1) * P],
                                                  state[:, scan_index(d, t), d, :], start=True, stop=True)
                        mm.then_inc(e_done, c.sig(e_done))

                    weights_of(0)
                    for t in range(lt):
                        if t + 1 < lt:
                            weights_of(t + 1)
                        pe.wait_ge(w_done, first + t + 1)
                        if first + t:
                            pe.wait_ge(n_add, first + t)
                        for d in range(2):
                            mm = nc.tensor.matmul(ps[:, 6, d * (HD + 1):(d + 1) * (HD + 1)], wexp[t % 2][:, d, :],
                                                  v_tok[:, t, :], start=True, stop=True)
                        mm.then_inc(n_done, c.sig(n_done))
                    pe.wait_ge(hr_ready, c.next(hr_ready))
                    for t in range(lt):
                        mm = nc.tensor.transpose(ps[:, 4 + t // 4, (t % 4) * P:(t % 4 + 1) * P], hwork[:, t, :], ident[:])
                    mm.then_inc(hr_done, c.sig(hr_done))
                    pe.wait_ge(hr_evac, c.next(hr_evac))
                over(pe, c)

                b = c.now(blk_done)
                with pe.Fori(0, KB // 2) as i:
                    step = {lo_done: 12, blk_done: 12}
                    if l == 0:
                        step.update({mod_full[0]: 48, mod_full[1]: 48, mod_done: 6})
                    c.enter(i, step)
                    for pr in range(6):
                        if l == 0:
                            mod_beside(pr % 2, b % 2)
                        product(0, b % 2, KB, (h_hi, h_lo), chunks)
                        product(1, (b + 1) % 2, UB, (u_hi[pr % 3], u_lo[pr % 3]), chunks)
                    c.leave(KB // 2)
                over(pe, c)

                pe.wait_ge(y_split, c.next(y_split, KB))

                def projection(k_blocks, a_hi, a_lo, mods):
                    b = c.now(blk_done)
                    with pe.Fori(0, KB // 2) as i:
                        step = {lo_done: 2, blk_done: 2, tr_done: 2}
                        if mods:
                            step.update({mod_full[0]: 16, mod_full[1]: 16, mod_done: 2})
                        c.enter(i, step)
                        for j in range(2):
                            if mods:
                                mod_beside(j, (b + j) % 2)
                            product(j, (b + j) % 2, k_blocks, (a_hi, a_lo), chunks)
                        for j in range(2):
                            pe.wait_ge(blk_out, c.now(blk_done, 1 - j))
                            turn_back(j, chunks)
                        c.leave(KB // 2)

                projection(KB, h_hi, h_lo, l == 0)
                over(pe, c)
                norm_turns(l)
                over(pe, c)

                for g, blocks in enumerate(FG):
                    mods = l == 0 and g < 2
                    b = c.now(blk_done)
                    with pe.Fori(0, blocks // 2) as i:
                        step = {lo_done: 4, blk_done: 4}
                        if mods:
                            step.update({mod_full[0]: 32, mod_full[1]: 32, mod_done: 4})
                        c.enter(i, step)
                        for j in range(4):
                            if mods:
                                mod_beside(j % 2, (b + j) % 2)
                            product(j % 2, (b + j) % 2, KB, (h_hi, h_lo), chunks)
                        c.leave(blocks // 2)
                    over(pe, c)
                    projection(blocks, f_hi, f_lo, l == 0 and g == 0)
                    over(pe, c)
                if l == 0:
                    norm_turns(0)
                    over(pe, c)

        @block.scalar
        def _(act):
            c = Count()

            def link(ins):
                ins.then_inc(a_step, c.sig(a_step))
                act.wait_ge(a_step, c.now(a_step))

            def high(slot):
                act.wait_ge(raw_full[slot], c.next(raw_full[slot], 16))
                nc.scalar.activation(w_hi[slot][:], raw[slot][:], ACT.Copy).then_inc(hi_done, c.sig(hi_done))

            def take(pieces, slot=None):
                act.wait_ge(blk_done, c.next(blk_done))
                if slot is not None:
                    high(slot)
                for n, piece in enumerate(pieces):
                    ins = piece()
                ins.then_inc(blk_out, c.sig(blk_out))

            def copy_out(dst, buf, chunks, func=ACT.Copy, rows=slice(0, P), **kw):
                return [lambda q=q, t0=t0, size=size: nc.scalar.activation(
                    dst[rows, t0:t0 + size], ps[rows, 2 * buf + q, 0:size], func, **kw)
                    for q, (t0, size) in enumerate(chunks)]

            def mod_out(layer, m, buf):
                return lambda: nc.scalar.activation(modv[layer][:, m, :], ps[:, 2 * buf + 1, 508:510], ACT.Identity,
                                                    bias=bmod[:, layer, m:m + 1] if isinstance(m, int)
                                                    else bmod[:, layer, bass.ds(m, 1)])

            def norm(t, dst):
                act.wait_ge(var_done, c.next(var_done))
                nc.scalar.activation(root[:, t:t + 1], aggr[:, t, 1:2], ACT.Sqrt, bias=eps[:]).then_inc(
                    root_done, c.sig(root_done))
                act.wait_ge(stat_done, c.next(stat_done))
                nc.scalar.activation(dst[:, t, :], res[:, t, :], ACT.Identity, scale=rstd[:, t:t + 1],
                                     bias=nmr[:, t:t + 1]).then_inc(normed, c.sig(normed))

            def modulated(l, shift, scale, ahead):
                n_t = NT if shift == SHIFT1 else tiles_of(l)
                for t in range(min(ahead, n_t)):
                    norm(t, xn)
                if l == 0 and shift == SHIFT1:
                    act.wait_ge(mod_ready, 1)
                for t in range(n_t):
                    if t + ahead < n_t:
                        norm(t + ahead, xn)
                    s = 0 if t < LT else 1
                    for half in range(2):
                        act.wait_ge(xt_done, c.next(xt_done))
                        if c.now(xt_act) >= 2:
                            act.wait_ge(h_ready, c.now(xt_act, 1))
                        for k in range(4):
                            kk = 4 * half + k
                            ins = nc.scalar.activation(mod32[half][:, k, :], ps[:, 4 + half, k * P:(k + 1) * P],
                                                       ACT.Identity, scale=modv[l][:, scale + kk, s:s + 1],
                                                       bias=modv[l][:, shift + kk, s:s + 1])
                        ins.then_inc(xt_act, c.sig(xt_act))

            def post_norm(n_t):
                for t in range(n_t):
                    norm(t, res)
                c.next(x_new, n_t)

            def load_x(l):
                for t in range(tiles_of(l)):
                    if l == 0:
                        src = x_lat[t * P:(t + 1) * P, :] if t < LT else ctx[(t - LT) * P:(t - LT + 1) * P, :]
                    else:
                        src = spill[t * P:(t + 1) * P, :]
                    act.dma_start(res[:, t, :], src).then_inc(x_in[t], 16)

            def load_gb(l, which):
                act.dma_start(ln_g[:], ln_gb[l, which:which + 1, :].partition_broadcast(P)).then_inc(tab_in, 16)
                act.dma_start(ln_b[:], ln_gb[l, which + 1:which + 2, :].partition_broadcast(P)).then_inc(tab_in, 16)

            act.dma_start(cin[:], cvec).then_inc(const_in, 16)
            load_x(0)
            for dst, src in ((bmod, b_mod), (vec, vecs), (sink, sinks), (ifb, ifbias), (ident, consts[0]),
                             (rot, consts[1]), (mask32, consts[2:4].rearrange("a p b -> p a b"))):
                act.dma_start(dst[:], src).then_inc(const_in, 16)
            act.wait_ge(const_in, CONST_ALL)
            nc.scalar.activation(cact[:], cin[:], ACT.Silu).then_inc(a_step, c.sig(a_step))
            high(0)
            high(1)
            modulated(0, SHIFT1, SCALE1, NT)
            over(act, c)
            for l in range(DEPTH):
                chunks = live(l)
                lt = tiles_of(l)
                width = chunks[-1][0] + chunks[-1][1]
                b0 = c.now(blk_out)
                if l:
                    for t in range(lt):
                        act.dma_start(spill[t * P:(t + 1) * P, :], res[:, t, :]).then_inc(stored, 16)
                    act.wait_ge(stored, c.next(stored, 16 * lt))
                for g in range(2):
                    act.dma_start(inv[g][:], pool_inv[g:g + 1, :].partition_broadcast(P)).then_inc(inv_in[g], 16)
                if l:
                    act.drain().then_inc(room, 1)
                for g in range(UB):
                    if g >= 2:
                        act.wait_ge(pu_ready, c.now(pu_ready) + g - 1)
                        act.dma_start(inv[g % 2][:], pool_inv[g:g + 1, :].partition_broadcast(P)).then_inc(inv_in[g % 2], 16)
                    buf = (b0 + g) % 2
                    a = apad[g % 2]
                    pieces = [lambda buf=buf, a=a: nc.scalar.activation(a[:, LAT0:LAT0 + SEQ], ps[:, 2 * buf, 0:SEQ], ACT.Copy)]
                    if len(chunks) > 1:
                        pieces.append(lambda buf=buf, a=a: nc.scalar.activation(a[:, CTX0:CTX0 + CTX], ps[:, 2 * buf + 1, 0:CTX], ACT.Copy))
                    if l == 0:
                        pieces.insert(0, mod_out(0, MODS_FIRST + g, buf))
                    if g == 0:
                        act.wait_ge(py_free, c.next(py_free))
                    take(pieces, g % 2)
                c.next(pu_ready, UB)
                buf = (b0 + UB) % 2
                take([lambda q=q, t0=t0, size=size, dst=dst, r0=r0, j=j, buf=buf: nc.scalar.activation(
                    dst[:, t0:t0 + size], ps[r0:r0 + ROWS, 2 * buf + q, 0:size], ACT.Identity, bias=ifb[:, l, j:j + 1])
                    for j, (dst, r0) in enumerate(((ig, 0), (fg, 64))) for q, (t0, size) in enumerate(ALL)], 0)
                for g in range(UB):
                    if g >= 2:
                        act.wait_ge(py_free, c.now(py_free) + g - 1)
                    take(copy_out(pool_y[g % 2], (b0 + UB + 1 + g) % 2, chunks, scale=vec[:, l, 0, g:g + 1]),
                         1 if g == UB - 1 else None)
                c.next(py_free, UB)
                over(act, c)

                act.dma_start(cos[:], tables[0]).then_inc(tab_in, 16)
                act.dma_start(sin[:], tables[1]).then_inc(tab_in, 16)
                take(copy_out(kT, 0, ALL), 0)
                take(copy_out(vT, 0, ALL), 1)
                for p in range(PAIRS):
                    if p:
                        act.wait_ge(at_evac, c.next(at_evac))
                    take(copy_out(qT, 0, chunks), p % 2)
                    U = units(l)
                    first = c.now(p_exp)

                    def exponentials(n):
                        i, x = U[n]
                        par = n % 2
                        nb = len(band(i))
                        act.wait_ge(s_max, first + n + 1)
                        if first + n >= 2:
                            act.wait_ge(pv_evac, first + n - 1)
                        if nb:
                            nc.scalar.activation(probs[par][:, 0:nb, :].rearrange("p a b -> p (a b)"),
                                                 ps[:, 4, 0:nb * P], ACT.Exp, scale=AH ** -0.5, bias=negm[:, par:par + 1])
                        head = p + PAIRS * x
                        nc.scalar.activation(esink[:, par:par + 1], negm[:, par:par + 1], ACT.Exp,
                                             bias=sink[:, l, head:head + 1])
                        nc.scalar.activation(probs[par][:, nb:nb + 2, :].rearrange("p a b -> p (a b)"),
                                             ps[:, 5, 0:CTX], ACT.Exp, scale=AH ** -0.5,
                                             bias=negm[:, par:par + 1]).then_inc(p_exp, c.sig(p_exp))

                    exponentials(0)
                    for n, (i, x) in enumerate(U):
                        par = n % 2
                        nk = len(keys(i))
                        act.wait_ge(pt_done, first + n + 1)
                        a_, b_ = min(nk, 4), nk - 4
                        ins = nc.scalar.activation(probsT[par][:, 0:a_, :].rearrange("p a b -> p (a b)"),
                                                   ps[:, 6, 0:a_ * P], ACT.Copy)
                        if b_ > 0:
                            ins = nc.scalar.activation(probsT[par][:, 4, :], ps[:, 7, 0:P], ACT.Copy)
                        ins.then_inc(pt_evac, c.sig(pt_evac))
                        if n + 1 < len(U):
                            exponentials(n + 1)
                over(act, c)
                c.next(at_evac)

                link(nc.scalar.activation(r_t[:], fg[:], ACT.Abs))
                link(nc.scalar.activation(r_a[:], r_t[:], ACT.Exp, scale=-1.0))
                nc.scalar.activation(r_b[:], r_a[:], ACT.Ln, bias=1.0).then_inc(row_act, c.sig(row_act))
                act.wait_ge(row_dve, c.next(row_dve))
                nc.scalar.activation(r_dec[:], r_dec[:], ACT.Exp)
                nc.scalar.activation(r_t[:], r_t[:], ACT.Exp)
                nc.scalar.activation(r_w[:], r_w[:], ACT.Exp)
                nc.scalar.activation(r_e[:], r_e[:], ACT.Exp, scale=-1.0).then_inc(row_act, c.sig(row_act))
                c.next(row_dve)
                act.wait_ge(row_evac, c.next(row_evac))
                for hd in range(HEADS):
                    b = c.now(blk_out)
                    if hd:
                        act.wait_ge(hr_evac, c.next(hr_evac))
                    take(copy_out(hq, b % 2, chunks), 0)
                    take(copy_out(hk, (b + 1) % 2, ALL, scale=HD ** -0.5), 1)
                    take(copy_out(hv, (b + 2) % 2, ALL), 0)
                    take(copy_out(ho, (b + 3) % 2, chunks, ACT.Sigmoid), 1)
                    act.wait_ge(kt_done, c.next(kt_done))
                    nc.scalar.activation(k_tok[:, 0:4, :].rearrange("p a b -> p (a b)"), ps[:, 6, :], ACT.Copy)
                    nc.scalar.activation(k_tok[:, 4:6, :].rearrange("p a b -> p (a b)"), ps[:, 7, 0:2 * P],
                                         ACT.Copy).then_inc(kt_evac, c.sig(kt_evac))
                    c.next(kt_done)
                    first = c.now(e_exp)
                    for t in range(lt):
                        act.wait_ge(e_done, c.next(e_done))
                        if first + t >= 2:
                            act.wait_ge(n_done, first + t - 1)
                        for d in range(2):
                            row = 32 * d + hd
                            ins = nc.scalar.activation(wexp[t % 2][:, d, :], ps[:, 4 + t % 2, d * P:(d + 1) * P], ACT.Exp,
                                                       bias=cols[:, t, 0, row:row + 1])
                        ins.then_inc(e_exp, c.sig(e_exp))
                        if first + t:
                            act.wait_ge(n_add, first + t)
                        for d in range(2):
                            row = 32 * d + hd
                            ins = nc.scalar.activation(inter[:, d, :], ps[:, 7, d * (HD + 1):(d + 1) * (HD + 1)], ACT.Copy,
                                                       scale=cols[:, t, 2, row:row + 1])
                        ins.then_inc(i_evac, c.sig(i_evac))
                    act.wait_ge(var_done, c.next(var_done))
                    nc.scalar.activation(hroot[:, 0:lt], haggr[:, 0:lt, 1], ACT.Sqrt, bias=eps[:]).then_inc(
                        root_done, c.sig(root_done))
                over(act, c)
                c.next(hr_evac)

                b = c.now(blk_out)
                with act.Fori(0, KB // 2) as i:
                    c.enter(i, {blk_done: 12, blk_out: 12, raw_full[0]: 96, raw_full[1]: 96, hi_done: 12, pair_free: 6})
                    for pr in range(6):
                        par = pr % 2
                        act.wait_ge(pair_free, c.next(pair_free))
                        pieces = copy_out(gated[par], b % 2, chunks, ACT.Sigmoid)
                        if l == 0:
                            pieces.insert(0, mod_out(0, i * 6 + (MODS_FIRST + UB + pr), b % 2))
                        take(pieces, 0)
                        take(copy_out(value[par], (b + 1) % 2, chunks), 1)
                    c.leave(KB // 2)
                over(act, c)

                act.wait_ge(y_split, c.next(y_split, KB))
                load_x(l)

                def projection(gate, mods, m0, end=False):
                    b = c.now(blk_out)

                    def two(i, ahead=True):
                        for j in range(2):
                            buf = (b + j) % 2
                            pieces = [lambda q=q, t0=t0, size=size, j=j, buf=buf: nc.scalar.activation(
                                y_out[j][:, t0:t0 + size], ps[:, 2 * buf + q, 0:size], ACT.Copy,
                                scale=gate_col(i * 2 + (gate + j), q)) for q, (t0, size) in enumerate(chunks)]
                            if mods:
                                pieces.insert(0, mod_out(1, i * 2 + (m0 + j), buf))
                            take(pieces, j if ahead else None)

                    def gate_col(m, q):
                        return modv[l][:, bass.ds(m, 1), q]

                    turns = KB // 2 - (1 if end else 0)
                    with act.Fori(0, turns) as i:
                        c.enter(i, {blk_done: 2, blk_out: 2, raw_full[0]: 16, raw_full[1]: 16, hi_done: 2})
                        two(i)
                        c.leave(turns)
                    if end:
                        two(turns, ahead=False)

                projection(GATE1, l == 0, 0)
                over(act, c)
                load_gb(l, 0)
                post_norm(lt)
                modulated(l, SHIFT2, SCALE2, 2)
                over(act, c)
                for g, blocks in enumerate(FG):
                    mods = l == 0 and g < 2
                    b = c.now(blk_out)
                    with act.Fori(0, blocks // 2) as i:
                        c.enter(i, {blk_done: 4, blk_out: 4, raw_full[0]: 32, raw_full[1]: 32, hi_done: 4, pair_free: 2})
                        for j in range(2):
                            act.wait_ge(pair_free, c.next(pair_free))
                            pieces = copy_out(gated[j], b % 2, chunks, ACT.Silu)
                            vals = copy_out(value[j], (b + 1) % 2, chunks)
                            if mods:
                                m0 = KB if g == 0 else KB + 3 * KB
                                pieces.insert(0, mod_out(1, i * 4 + (m0 + 2 * j), b % 2))
                                vals.insert(0, mod_out(1, i * 4 + (m0 + 2 * j + 1), (b + 1) % 2))
                            take(pieces, 0)
                            take(vals, 1)
                        c.leave(blocks // 2)
                    over(act, c)
                    last_group = l == DEPTH - 1 and g == len(FG) - 1
                    projection(GATE2, l == 0 and g == 0, 3 * KB, end=last_group)
                    over(act, c)
                load_gb(l, 2)
                post_norm(lt)
                if l == 0:
                    modulated(1, SHIFT1, SCALE1, 2)
                    over(act, c)
            for t in range(LT):
                act.wait_ge(x_new, c.now(x_new) - LT + t + 1)
                act.dma_start(out[t * P:(t + 1) * P, :], res[:, t, :]).then_inc(stored, 16)
            act.wait_ge(stored, c.next(stored, 16 * LT))

        @block.vector
        def _(dve):
            c = Count()
            v = nc.vector

            def link(ins):
                ins.then_inc(v_step, c.sig(v_step))
                dve.wait_ge(v_step, c.now(v_step))

            def statistics(t, loaded=False):
                if loaded:
                    dve.wait_ge(x_in[t], c.next(x_in[t], 16))
                for half in range(2):
                    ins = v.bn_stats(stats[:, t, half, :], res[:, t, half * 512:(half + 1) * 512])
                link(ins)
                v.bn_aggr(aggr[:, t, :], stats[:, t, :, :].rearrange("p a b -> p (a b)")).then_inc(
                    var_done, c.sig(var_done))
                dve.wait_ge(var_done, c.now(var_done))
                dve.wait_ge(root_done, c.next(root_done))
                link(v.reciprocal(rstd[:, t:t + 1], root[:, t:t + 1]))
                v.tensor_scalar(nmr[:, t:t + 1], aggr[:, t, 0:1], rstd[:, t:t + 1], -1.0, ALU.mult,
                                ALU.mult).then_inc(stat_done, c.sig(stat_done))

            def halves(t):
                for half in range(2):
                    dve.wait_ge(xt_act, c.next(xt_act))
                    hi = h_hi[:, 4 * half:4 * half + 4, t * P:(t + 1) * P]
                    link(v.tensor_copy(hi, mod32[half][:]))
                    v.tensor_tensor(h_lo[:, 4 * half:4 * half + 4, t * P:(t + 1) * P], mod32[half][:],
                                    hi.bitcast(F32), ALU.subtract).then_inc(h_ready, c.sig(h_ready))

            def modulated(n_t, ahead, loaded=False):
                for t in range(min(ahead, n_t)):
                    statistics(t, loaded)
                if loaded:
                    dve.wait_ge(mod_done, c.next(mod_done, MODS_FIRST))
                    v.tensor_tensor(modv[0][:, 0:MODS_FIRST, :],
                                    ps[:, 6, 0:2 * MODS_FIRST].rearrange("p (a b) -> p a b", b=2),
                                    bmod[:, 0, 0:MODS_FIRST].unsqueeze(2).broadcast_to([P, MODS_FIRST, 2]),
                                    ALU.add).then_inc(mod_ready, 1)
                for t in range(n_t):
                    if t + ahead < n_t:
                        statistics(t + ahead, loaded)
                    halves(t)

            def post_norm(n_t):
                def gain(t):
                    dve.wait_ge(normed, c.next(normed))
                    link(v.tensor_tensor(res[:, t, :], res[:, t, :], ln_g[:], ALU.mult))
                    v.tensor_tensor(res[:, t, :], res[:, t, :], ln_b[:], ALU.add).then_inc(x_new, c.sig(x_new))

                statistics(0)
                statistics(1)
                dve.wait_ge(tab_in, c.next(tab_in, 32))
                for t in range(n_t):
                    gain(t)
                    if t + 2 < n_t:
                        statistics(t + 2)
                dve.wait_ge(x_new, c.now(x_new))

            dve.wait_ge(const_in, CONST_ALL)
            v.memset(eps[:], EPS)
            v.tensor_copy(ident16[:], ident[:])
            v.tensor_copy(mask16[:], mask32[:])
            v.tensor_scalar(negsink[:], sink[:], -1.0, None, ALU.mult)
            for first in (SCALE1, SCALE2):
                ins = v.tensor_scalar(bmod[:, :, first:first + KB], bmod[:, :, first:first + KB], 1.0, None, ALU.add)
            link(ins)
            modulated(NT, NT, loaded=True)
            c.next(normed, NT)
            dve.drain().then_inc(pair_free, c.sig(pair_free, 2))
            dve.drain().then_inc(tr_free, c.sig(tr_free, 2))
            over(dve, c)
            for l in range(DEPTH):
                chunks = live(l)
                lt = tiles_of(l)
                tok = lt * P
                width = PW if len(chunks) > 1 else LATW
                segments = [(0, SEQ, LAT0), (SEQ, CTX, CTX0)][:len(chunks)]

                if l:
                    dve.wait_ge(room, 1)
                v.memset(apad[0][:], 0.0)
                v.memset(apad[1][:], 0.0).then_inc(py_free, c.sig(py_free))
                dve.wait_ge(py_free, c.now(py_free))
                products = c.now(blk_out) + UB + 1
                for g in range(UB):
                    w = WINDOWS[g]
                    a = apad[g % 2]
                    dve.wait_ge(blk_out, c.next(blk_out))
                    dve.wait_ge(inv_in[g % 2], c.next(inv_in[g % 2], 16))
                    src = a
                    for k in range(g + 1):
                        dst = sums[k % 2]
                        n = width - (2 ** (k + 1) - 1)
                        link(v.tensor_tensor(dst[:, 0:n], src[:, 0:n], src[:, 2 ** k:2 ** k + n], ALU.add))
                        src = dst
                    mean = sums[(g + 1) % 2]
                    n = width - 2 * PAD
                    link(v.tensor_tensor(mean[:, PAD:PAD + n], src[:, PAD - w // 2:PAD - w // 2 + n],
                                         inv[g % 2][:, PAD:PAD + n], ALU.mult))
                    for t0, size, at_ in segments:
                        ins = v.tensor_tensor(pool_u[:, t0:t0 + size], mean[:, at_:at_ + size], a[:, at_:at_ + size],
                                              ALU.subtract)
                    link(ins)
                    if g >= 2:
                        dve.wait_ge(blk_out, products + g - 1)
                    link(v.tensor_copy(pu_hi[g % 2][:, 0:tok], pool_u[:, 0:tok]))
                    v.tensor_tensor(pu_lo[g % 2][:, 0:tok], pool_u[:, 0:tok], pu_hi[g % 2][:, 0:tok].bitcast(F32),
                                    ALU.subtract).then_inc(pu_ready, c.sig(pu_ready))
                c.next(blk_out)
                for g in range(UB):
                    dve.wait_ge(blk_out, c.next(blk_out))
                    hi = u_hi[0][:, g, 0:tok]
                    link(v.tensor_copy(hi, pool_y[g % 2][:, 0:tok]))
                    v.tensor_tensor(u_lo[0][:, g, 0:tok], pool_y[g % 2][:, 0:tok], hi.bitcast(F32),
                                    ALU.subtract).then_inc(py_free, c.sig(py_free))
                over(dve, c)

                v.memset(vaug[:, :, :, AH:AH + 1], 1.0)
                dve.wait_ge(tab_in, c.next(tab_in, 32))

                def rotated(z):
                    dve.wait_ge(rot_done, c.next(rot_done))
                    v.tensor_tensor(rope_c[:], z[:, 0:SEQ], cos[:], ALU.mult)
                    link(v.tensor_tensor(rope_s[:], ps[:, 3, :], sin[:], ALU.mult))
                    v.tensor_tensor(z[:, 0:SEQ], rope_c[:], rope_s[:], ALU.add).then_inc(rope_done, c.sig(rope_done))

                rotated(kT)
                dve.wait_ge(vt_done, c.next(vt_done))
                v.tensor_copy(vaug[:, 0:4, :, 0:AH], ps[:, 6, :].rearrange("p (a b d) -> p a b d", a=4, b=2))
                v.tensor_copy(vaug[:, 4:6, :, 0:AH], ps[:, 7, 0:2 * P].rearrange(
                    "p (a b d) -> p a b d", a=2, b=2)).then_inc(vt_evac, c.sig(vt_evac))
                for p in range(PAIRS):
                    dve.wait_ge(rope_done, c.now(rope_done))
                    rotated(qT)
                    U = units(l)

                    def maxima(n):
                        i, x = U[n]
                        par = n % 2
                        head = p + PAIRS * x
                        nb = len(band(i))
                        dve.wait_ge(s_done, c.next(s_done))
                        m = mx[:, par, 1:2]
                        if nb:
                            v.reduce_max(mx[:, par, 0:1], ps[:, 4, 0:nb * P], AX_X)
                        link(v.reduce_max(m, ps[:, 5, 0:CTX], AX_X))
                        if nb:
                            link(v.tensor_tensor(mrow[:, par:par + 1], mx[:, par, 0:1], m, ALU.max))
                            m = mrow[:, par:par + 1]
                        v.tensor_scalar(negm[:, par:par + 1], m, -(AH ** -0.5), negsink[:, l, head:head + 1],
                                        ALU.mult, ALU.min).then_inc(s_max, c.sig(s_max))

                    def output(n):
                        i, x = U[n]
                        par = n % 2
                        dve.wait_ge(pv_done, c.next(pv_done))
                        link(v.tensor_tensor(den[:, par:par + 1], ps[:, 2, AH:AH + 1], esink[:, par:par + 1], ALU.add))
                        link(v.reciprocal(rden[:, par:par + 1], den[:, par:par + 1]))
                        v.tensor_scalar(att[:, i, AH * x:AH * x + AH], ps[:, 2, 0:AH], rden[:, par:par + 1], None,
                                        ALU.mult).then_inc(pv_evac, c.sig(pv_evac))

                    maxima(0)
                    for n in range(len(U)):
                        if n + 1 < len(U):
                            maxima(n + 1)
                        output(n)
                    dve.wait_ge(at_done, c.next(at_done))
                    for q, (t0, size) in enumerate(chunks):
                        ins = v.tensor_copy(u_hi[2][:, p, t0:t0 + size], ps[:, 6 + q, 0:size])
                    link(ins)
                    for q, (t0, size) in enumerate(chunks):
                        ins = v.tensor_tensor(u_lo[2][:, p, t0:t0 + size], ps[:, 6 + q, 0:size],
                                              u_hi[2][:, p, t0:t0 + size].bitcast(F32), ALU.subtract)
                    ins.then_inc(at_evac, c.sig(at_evac))
                over(dve, c)

                def reorder(dst, src, back=False, by=None):
                    for rows, rev in ((slice(0, 32), False), (slice(32, ROWS), True)):
                        for natural, scan in ((slice(SEQ, TOK), slice(0, CTX)), (slice(0, SEQ), slice(CTX, TOK))):
                            a_, b_ = (scan, natural) if back else (natural, scan)
                            s_ = src[rows, a_]
                            if rev:
                                s_ = s_[:, ::-1]
                            if by is None:
                                ins = v.tensor_copy(dst[rows, b_], s_)
                            else:
                                ins = v.tensor_scalar(dst[rows, b_], s_, by, None, ALU.mult)
                    return ins

                v.memset(zeros[:], 0.0)
                v.memset(m_in[:, 0:1], 0.0)
                dve.wait_ge(row_act, c.next(row_act))
                link(v.scalar_tensor_tensor(r_m[:], fg[:], 0.0, r_b[:], ALU.min, ALU.subtract))
                reorder(r_i, ig)
                link(reorder(r_w, r_m))
                for s in range(NT):
                    cs = slice(s * P, (s + 1) * P)
                    ins = v.tensor_tensor_scan(r_b[:, cs], r_w[:, cs], zeros[:], 0.0, ALU.add, ALU.add)
                link(ins)
                link(v.tensor_tensor(r_a[:], r_i[:], r_b[:], ALU.subtract))
                for s in range(NT):
                    cs = slice(s * P, (s + 1) * P)
                    end = slice((s + 1) * P - 1, (s + 1) * P)
                    link(v.tensor_tensor_scan(r_m[:, cs], r_a[:, cs], r_a[:, cs], m_in[:, s:s + 1], ALU.max, ALU.max))
                    link(v.tensor_tensor(m_in[:, s + 1:s + 2], r_b[:, end], r_m[:, end], ALU.add))

                def by_chunk(r):
                    return r[:].rearrange("p (a b) -> p a b", b=P)

                ends = by_chunk(r_m)[:, :, P - 1:P]
                v.tensor_tensor(r_dec[:].unsqueeze(2), m_in[:, 0:NT].unsqueeze(2), ends, ALU.subtract)
                v.tensor_tensor(by_chunk(r_t), m_in[:, 0:NT].unsqueeze(2).broadcast_to([ROWS, NT, P]), by_chunk(r_m),
                                ALU.subtract)
                v.tensor_tensor(by_chunk(r_w), by_chunk(r_a), ends.broadcast_to([ROWS, NT, P]), ALU.subtract)
                v.tensor_tensor(r_e[:], r_b[:], r_m[:], ALU.add).then_inc(row_dve, c.sig(row_dve))
                reorder(n_row[0], r_a, back=True)
                reorder(neg_m, r_m, back=True, by=-1.0)
                dve.wait_ge(row_act, c.next(row_act))
                for q, r_ in ((1, r_w), (2, r_t), (3, r_e)):
                    ins = reorder(n_row[q], r_, back=True)
                ins.then_inc(row_dve, c.sig(row_dve))
                dve.wait_ge(row_pe, c.next(row_pe))
                for half in range(2):
                    v.tensor_copy(cols[:, 3 * half:3 * half + 3, :, :].rearrange("p a b d -> p (a b d)"),
                                  ps[:, 4 + half, 0:12 * ROWS])
                v.tensor_copy(decay[:].rearrange("p a b -> p (a b)"), ps[:, 6, 0:2 * HEADS * NT]).then_inc(
                    row_evac, c.sig(row_evac))
                dve.wait_ge(row_evac, c.now(row_evac))
                v.memset(v_tok[:, :, HD:HD + 1], 1.0)
                link(v.memset(state[:, 0, :, :], 0.0))
                for hd in range(HEADS):
                    dve.wait_ge(kt_done, c.next(kt_done, 2))
                    v.tensor_copy(v_tok[:, 0:4, 0:HD], ps[:, 4, :].rearrange("p (a b) -> p a b", b=HD))
                    v.tensor_copy(v_tok[:, 4:6, 0:HD], ps[:, 5, 0:2 * HD].rearrange("p (a b) -> p a b", b=HD)).then_inc(
                        v_evac, c.sig(v_evac))
                    dve.wait_ge(v_evac, c.now(v_evac))

                    def gated_v(n):
                        s, d = STATES[n]
                        t = chunk_at(d, s)
                        if n >= 2:
                            dve.wait_ge(st_done, c.now(st_done) + n - 1)
                        row = 32 * d + hd
                        v.tensor_scalar(vw[d][:], v_tok[:, t, :], cols[:, t, 1, row:row + 1], None,
                                        ALU.mult).then_inc(vw_done, c.sig(vw_done))

                    gated_v(0)
                    gated_v(1)
                    for n, (s, d) in enumerate(STATES):
                        dve.wait_ge(st_done, c.now(st_done) + n + 1)
                        v.scalar_tensor_tensor(state[:, s + 1, d, :], state[:, s, d, :],
                                               decay[:, HEADS * d + hd, s:s + 1], ps[:, 6 + d, 0:HD + 1],
                                               ALU.mult, ALU.add).then_inc(st_step, c.sig(st_step))
                        if n + 2 < len(STATES):
                            gated_v(n + 2)
                        if n:
                            dve.wait_ge(st_step, c.now(st_step, 1))
                    dve.wait_ge(st_step, c.now(st_step))
                    c.next(st_done, len(STATES))

                    def decayed(t):
                        dve.wait_ge(e_exp, c.next(e_exp))
                        v.tensor_tensor(wexp[t % 2][:], wexp[t % 2][:],
                                        ps[:, 4 + t % 2, 2 * P:3 * P].unsqueeze(1).broadcast_to([P, 2, P]),
                                        ALU.mult).then_inc(w_done, c.sig(w_done))

                    decayed(0)
                    for t in range(lt):
                        if t + 1 < lt:
                            decayed(t + 1)
                        dve.wait_ge(n_done, c.next(n_done))
                        dve.wait_ge(i_evac, c.next(i_evac))
                        v.tensor_tensor(total[:, t, :, :], ps[:, 6, 0:2 * (HD + 1)].rearrange("p (a b) -> p a b", a=2),
                                        inter[:], ALU.add).then_inc(n_add, c.sig(n_add))
                    dve.wait_ge(n_add, c.now(n_add))
                    bound = cols[:, 0:lt, 3, hd:hd + 33:32]
                    nq, most = total[:, 0:lt, :, HD], denr[:, 0:lt, :]
                    link(v.scalar_tensor_tensor(most, nq, -1.0, nq, ALU.mult, ALU.max))
                    link(v.tensor_tensor(most, most, bound, ALU.max))
                    link(v.reciprocal(rdenr[:, 0:lt, :], denr[:, 0:lt, :]))
                    link(v.tensor_tensor(total[:, 0:lt, :, 0:HD], total[:, 0:lt, :, 0:HD],
                                         rdenr[:, 0:lt, :].unsqueeze(3).broadcast_to([P, lt, 2, HD]), ALU.mult))
                    link(v.tensor_tensor(hwork[:, 0:lt, :], total[:, 0:lt, 0, 0:HD], total[:, 0:lt, 1, 0:HD], ALU.add))
                    for t in range(lt):
                        ins = v.bn_stats(hstat[:, t, :], hwork[:, t, :])
                    link(ins)
                    for t in range(lt):
                        ins = v.bn_aggr(haggr[:, t, :], hstat[:, t, :])
                    ins.then_inc(var_done, c.sig(var_done))
                    dve.wait_ge(var_done, c.now(var_done))
                    dve.wait_ge(root_done, c.next(root_done))
                    link(v.reciprocal(hrstd[:, 0:lt], hroot[:, 0:lt]))
                    for t in range(lt):
                        ins = v.tensor_scalar(hwork[:, t, :], hwork[:, t, :], haggr[:, t, 0:1], hrstd[:, t:t + 1],
                                              ALU.subtract, ALU.mult)
                    ins.then_inc(hr_ready, c.sig(hr_ready))
                    dve.wait_ge(hr_done, c.next(hr_done))
                    dve.wait_ge(blk_out, BLOCKS * l + 15 + 4 * (hd + 1))
                    for q, (t0, size) in enumerate(chunks):
                        ins = v.scalar_tensor_tensor(hv[:, t0:t0 + size], ps[:, 4 + q, 0:size], vec[:, l, 1, hd:hd + 1],
                                                     ho[:, t0:t0 + size], ALU.mult, ALU.mult)
                    link(ins)
                    hi = u_hi[1][:, hd, 0:tok]
                    link(v.tensor_copy(hi, hv[:, 0:tok]))
                    v.tensor_tensor(u_lo[1][:, hd, 0:tok], hv[:, 0:tok], hi.bitcast(F32),
                                    ALU.subtract).then_inc(hr_evac, c.sig(hr_evac))
                over(dve, c)
                c.next(blk_out, 2 + PAIRS + 4 * HEADS)

                with dve.Fori(0, KB // 2) as i:
                    c.enter(i, {blk_out: 12, pair_free: 6, v_step: 4})
                    for pr in range(6):
                        dve.wait_ge(blk_out, c.next(blk_out, 2))
                        y = y32[:, i * 2 + pr // 3, 0:tok]
                        to = y if pr % 3 == 0 else prod[:, 0:tok]
                        v.tensor_tensor(to, gated[pr % 2][:, 0:tok], value[pr % 2][:, 0:tok], ALU.mult).then_inc(
                            pair_free, c.sig(pair_free))
                        dve.wait_ge(pair_free, c.now(pair_free))
                        if pr % 3:
                            link(v.tensor_tensor(y, y, prod[:, 0:tok], ALU.add))
                    c.leave(KB // 2)
                for k in range(KB):
                    link(v.tensor_copy(h_hi[:, k, 0:tok], y32[:, k, 0:tok])) if k else None
                    if k == 0:
                        over(dve, c)
                        link(v.tensor_copy(h_hi[:, k, 0:tok], y32[:, k, 0:tok]))
                    v.tensor_tensor(h_lo[:, k, 0:tok], y32[:, k, 0:tok], h_hi[:, k, 0:tok].bitcast(F32),
                                    ALU.subtract).then_inc(y_split, c.sig(y_split))

                def residual(alpha):
                    with dve.Fori(0, KB // 2) as i:
                        c.enter(i, {tr_done: 2, tr_free: 2})
                        for j in range(2):
                            dve.wait_ge(tr_done, c.next(tr_done))
                            for q, (t0, size) in enumerate(chunks):
                                t_ = t0 // P
                                r_ = res[:, t_:t_ + size // P, bass.ds(i * (2 * P) + j * P, P)]
                                ins = v.scalar_tensor_tensor(
                                    r_, r_, alpha, ps[:, 4 + 2 * j + q, 0:size].rearrange("p (a b) -> p a b", b=P),
                                    ALU.mult, ALU.add)
                            ins.then_inc(tr_free, c.sig(tr_free))
                        c.leave(KB // 2)

                for t in range(lt):
                    dve.wait_ge(x_in[t], c.next(x_in[t], 16))
                residual(ALPHA)
                c.next(blk_out, KB)
                over(dve, c)
                post_norm(lt)
                modulated(lt, 2)
                c.next(normed, lt)
                over(dve, c)

                for g, blocks in enumerate(FG):
                    with dve.Fori(0, blocks // 2) as i:
                        c.enter(i, {blk_out: 4, pair_free: 2, v_step: 4})
                        for j in range(2):
                            dve.wait_ge(blk_out, c.next(blk_out, 2))
                            v.tensor_tensor(prod[:, 0:tok], gated[j][:, 0:tok], value[j][:, 0:tok],
                                            ALU.mult).then_inc(pair_free, c.sig(pair_free))
                            dve.wait_ge(pair_free, c.now(pair_free))
                            hi = f_hi[:, i * 2 + j, 0:tok]
                            link(v.tensor_copy(hi, prod[:, 0:tok]))
                            link(v.tensor_tensor(f_lo[:, i * 2 + j, 0:tok], prod[:, 0:tok], hi.bitcast(F32),
                                                 ALU.subtract))
                        c.leave(blocks // 2)
                    over(dve, c)
                    residual(ALPHA if g == 0 else 1.0)
                    c.next(blk_out, KB)
                    over(dve, c)
                post_norm(lt)
                if l == 0:
                    modulated(NT, 2)
                    c.next(normed, NT)
                    over(dve, c)


def constants():
    ident = np.eye(P, dtype=np.float32)
    rot = np.zeros((P, P), np.float32)
    for f in range(P):
        if f % 32 < 16:
            rot[f + 16, f] = -1.0
        else:
            rot[f - 16, f] = 1.0
    row, col = np.arange(P)[:, None], np.arange(P)[None, :]
    before = np.where(col < row, np.float32(MASKED), np.float32(0))
    after = np.where(col > row, np.float32(MASKED), np.float32(0))
    consts = np.stack([ident, rot, before, after]).astype(np.float32)
    grid_w, pairs = 64, AH // 4
    inv = np.float32(10000.0) ** (-np.arange(pairs, dtype=np.float32) / np.float32(pairs))
    t = np.arange(SEQ)
    axes = ((t // grid_w).astype(np.float32), (t % grid_w).astype(np.float32))
    ang = np.concatenate([np.concatenate([a[:, None] * inv] * 2, axis=1) for a in axes], axis=1).T
    ang = np.concatenate([ang, ang], axis=0).astype(np.float32)
    tables = np.stack([np.cos(ang), np.sin(ang)]).astype(np.float32)
    inverse = np.zeros((UB, PW), np.float32)
    for g, w in enumerate(WINDOWS):
        for n, at in ((SEQ, LAT0), (CTX, CTX0)):
            tt = np.arange(n)
            count = np.clip(tt - w // 2 + w, 0, n) - np.clip(tt - w // 2, 0, n)
            inverse[g, at:at + n] = np.float32(1) / count.astype(np.float32)
    return consts, tables, inverse


def blocks_of(w):
    k, m = w.shape[0] // P, w.shape[1] // P
    return w.reshape(k, P, m, P).transpose(2, 1, 0, 3).reshape(m, P, k * P)


def widened(tiles):
    if tiles.shape[-1] == KB * P:
        return tiles
    out = np.zeros(tiles.shape[:-1] + (KB * P,), tiles.dtype)
    out[..., :tiles.shape[-1]] = tiles
    return out


def layer_tiles(w_in, pool_w, w_branch, w_out, w_gate, w_up, w_down):
    sizes = (BW, BW, BW, BW, BW, 2 * HEADS, 2 * HEADS, BW, P, P, 3 * D)
    a, q, k, v, o, ig, fg, qa, ka, va, gates = np.split(w_in, np.cumsum(sizes)[:-1], axis=1)
    rows = np.zeros((D, P), w_in.dtype)
    for n, part in enumerate((ig, fg)):
        for d in range(2):
            rows[:, 64 * n + 32 * d:64 * n + 32 * d + HEADS] = part[:, HEADS * d:HEADS * (d + 1)]
    qa = qa.reshape(D, 2, PAIRS, AH).transpose(0, 2, 1, 3).reshape(D, BW)
    tiles = [blocks_of(a), blocks_of(rows), widened(pool_w.transpose(1, 0, 2).reshape(1, P, UB * P)),
             blocks_of(ka), blocks_of(va), blocks_of(qa)]
    parts = [blocks_of(z) for z in (q, k, v, o)]
    tiles += [np.stack([z[h] for z in parts]) for h in range(HEADS)]
    branch = [w_branch[0], w_branch[1],
              w_branch[2].reshape(2, PAIRS, AH, D).transpose(1, 0, 2, 3).reshape(BW, D)]
    g = blocks_of(gates).reshape(3, KB, P, KB * P)
    b = np.stack([widened(blocks_of(z)) for z in branch])
    tiles += [np.stack([g, b], axis=2).transpose(1, 0, 2, 3, 4).reshape(6 * KB, P, KB * P)]
    tiles += [blocks_of(w_out)]
    gate, up = blocks_of(w_gate), blocks_of(w_up)
    at = 0
    for n in FG:
        tiles += [np.stack([gate[at:at + n], up[at:at + n]], axis=1).reshape(2 * n, P, KB * P),
                  widened(blocks_of(w_down[at * P:(at + n) * P]))]
        at += n
    return np.concatenate(tiles)


def by_partition(z):
    z = z.reshape(z.shape[:-1] + (-1, P))
    return np.ascontiguousarray(np.moveaxis(z, -1, 0))


def kernel(x, c, ctx, c_ctx, w_mod, b_mod, w_in, pool_w, pool_scale, m_b_i, m_b_f, m_norm_w, attn_sink, w_branch,
           w_out, ln1_g, ln1_b, ln2_g, ln2_b, w_ffn_gate, w_ffn_up, w_ffn_down):
    import concourse.bacc as bacc
    from concourse.bass_utils import run_bass_kernel_spmd

    a = {n: np.asarray(z) for n, z in dict(
        x=x, c=c, ctx=ctx, c_ctx=c_ctx, w_mod=w_mod, b_mod=b_mod, w_in=w_in, pool_w=pool_w, pool_scale=pool_scale,
        m_b_i=m_b_i, m_b_f=m_b_f, m_norm_w=m_norm_w, attn_sink=attn_sink, w_branch=w_branch, w_out=w_out,
        ln1_g=ln1_g, ln1_b=ln1_b, ln2_g=ln2_g, ln2_b=ln2_b, w_ffn_gate=w_ffn_gate, w_ffn_up=w_ffn_up,
        w_ffn_down=w_ffn_down).items()}
    consts, tables, inverse = constants()
    rows = np.zeros((ROWS, DEPTH, 2), np.float32)
    for n, bias in enumerate((a["m_b_i"], a["m_b_f"])):
        for d in range(2):
            rows[32 * d:32 * d + HEADS, :, n] = bias[:, d].T
    arrays = {
        "x_lat": a["x"].reshape(SEQ, D),
        "ctx": a["ctx"].reshape(CTX, D),
        "cvec": by_partition(np.stack([a["c"].reshape(D), a["c_ctx"]])).transpose(0, 2, 1),
        "w_mod": np.concatenate([blocks_of(a["w_mod"][l]) for l in range(DEPTH)]),
        "b_mod": by_partition(a["b_mod"]),
        "w_tiles": np.concatenate([layer_tiles(*(a[n][l] for n in (
            "w_in", "pool_w", "w_branch", "w_out", "w_ffn_gate", "w_ffn_up", "w_ffn_down"))) for l in range(DEPTH)]),
        "vecs": by_partition(np.stack([a["pool_scale"], a["m_norm_w"]], axis=1)),
        "ifbias": rows,
        "sinks": np.ascontiguousarray(np.broadcast_to(a["attn_sink"].reshape(1, DEPTH, 8), (P, DEPTH, 8))),
        "ln_gb": np.stack([a["ln1_g"], a["ln1_b"], a["ln2_g"], a["ln2_b"]], axis=1),
        "consts": consts,
        "tables": tables,
        "pool_inv": inverse,
    }
    arrays = {n: np.ascontiguousarray(z) for n, z in arrays.items()}
    nc = bacc.Bacc("TRN2", target_bir_lowering=False, num_devices=1)
    args = {n: nc.dram_tensor(n, z.shape, mybir.dt.from_np(z.dtype), kind="ExternalInput").ap()
            for n, z in arrays.items()}
    out = nc.dram_tensor("out", (SEQ, D), F32, kind="ExternalOutput").ap()
    trunk(nc, out=out, **args)
    result = run_bass_kernel_spmd(nc, [arrays], core_ids=[0])
    return result.results[0]["out"].reshape(1, SEQ, D)
```

```python
from contextlib import ExitStack

import numpy as np

import concourse.bass as bass
from concourse import mybir

ALU = mybir.AluOpType
ACT = mybir.ActivationFunctionType
F32 = mybir.dt.float32
F32R = mybir.dt.float32r
BF16 = mybir.dt.bfloat16
AX_X = mybir.AxisListType.X

P = 128
D = 1024
SEQ = 512
CTX = 256
TOK = SEQ + CTX
DEPTH = 2
KB = D // P
NT = TOK // P
LT = SEQ // P
BW = D // 2
UB = BW // P
HEADS = 4
HD = 128
AH = 64
PAIRS = 4
FF = 2816
FB = FF // P
FG = [8, 8, 6]
MB = 6 * KB
SHIFT1, SCALE1, GATE1, SHIFT2, SCALE2, GATE2 = (KB * i for i in range(6))
ALPHA = (2 * DEPTH) ** 0.25
EPS = 1e-5
MASKED = -1e30
PAD = 8
LAT0 = PAD
CTX0 = LAT0 + SEQ + 2 * PAD
PW = CTX0 + CTX + PAD
LATW = LAT0 + SEQ + PAD
SBUF_START, SBUF_END = 16512, 229344
WINDOWS = (2, 4, 8, 16)
MODS_FIRST = 2 * KB
FIRST_RING = 8
IN_TILES = 28
LAYER_TILES = IN_TILES + 48 + KB + sum(2 * g + KB for g in FG)
BLOCKS = 9 + 2 + 4 * HEADS + 6 * KB + KB + sum(2 * g + KB for g in FG)
CONST_ALL, LATE_ALL = 16 * 4, 16 * 3
PART = 3 * KB
HALF = KB // 2
ROWS = 36
ALL = ((0, SEQ), (SEQ, CTX))
LATENT = ((0, SEQ),)


class Count:

    def __init__(self):
        self.n, self.reg, self.step = {}, None, {}

    def next(self, sem, k=1):
        self.n[sem.name] = self.n.get(sem.name, 0) + k
        return self.now(sem)

    def now(self, sem, back=0):
        v = self.n.get(sem.name, 0) - back
        s = self.step.get(sem.name, 0)
        return self.reg * s + v if self.reg is not None and s else v

    def sig(self, sem, k=1):
        self.n[sem.name] = self.n.get(sem.name, 0) + k
        return k

    def enter(self, reg, step):
        self.reg, self.step = reg, {s.name: k for s, k in step.items()}
        self.at = dict(self.n)

    def leave(self, times):
        for name, v in self.n.items():
            per = v - self.at.get(name, 0)
            assert per == self.step.get(name, 0), (name, per, self.step.get(name, 0))
            self.n[name] = self.at.get(name, 0) + per * times
        self.reg, self.step = None, {}


def trunk(nc, x_lat, ctx, cvec, c_lines, w_mod, b_mod, w_tiles, vecs, ifbias, sinks, ln_gb, consts, tables, pool_inv, out):
    with ExitStack() as stack:
        def sem(name):
            return stack.enter_context(nc.semaphore(name))

        cursor = [SBUF_START]

        def place(name, shape, dt=F32, at=None):
            size = (int(np.prod(shape[1:])) * (2 if dt == BF16 else 4) + 31) // 32 * 32
            spot = cursor if at is None else at
            t = nc.alloc_sbuf_tensor_at(name, list(shape), dt, offset=spot[0])
            spot[0] += size
            assert spot[0] <= (SBUF_END if at is None else at[1]), (name, spot)
            return t

        def region(size):
            start = cursor[0]
            cursor[0] += size
            return start, start + size

        raw = [place(f"raw{i}", [P, KB, P]) for i in range(2)]
        w_hi = [place(f"w_hi{i}", [P, KB, P], F32R) for i in range(2)]
        w_lo = [place(f"w_lo{i}", [P, KB, P], F32R) for i in range(2)]
        mod_raw = [place(f"mod_raw{i}", [P, KB, P]) for i in range(2)]
        h_hi = place("h_hi", [P, KB, TOK], F32R)
        h_lo = place("h_lo", [P, KB, TOK], F32R)
        ident = place("ident", [P, P])
        rot = place("rot", [P, P])
        ident16 = place("ident16", [P, P], BF16)
        mask16 = place("mask16", [P, 2, P], BF16)
        modv = [place(f"modv{i}", [P, MB, 2]) for i in range(DEPTH)]
        bmod = place("bmod", [P, DEPTH, MB])
        vec = place("vec", [P, DEPTH, 2, UB])
        ifb = place("ifb", [ROWS, DEPTH, 2])
        sink = place("sink", [P, DEPTH, 8])
        negsink = place("negsink", [P, DEPTH, 8])
        cin = place("cin", [P, KB, 2])
        mod_sum = place("mod_sum", [P, 2, 2])
        cact = place("cact", [P, KB, 2])
        stats = place("stats", [P, NT, KB, 6])
        aggr = place("aggr", [P, NT, 2])
        rstd = place("rstd", [P, NT])
        nmr = place("nmr", [P, NT])
        root = place("root", [P, NT])
        eps = place("eps", [P, 1])
        idle = place("idle", [P, 1])
        u_region = region(3 * 2 * UB * TOK * 4)
        x_region = region(NT * D * 4)
        t_region = (cursor[0], SBUF_END)

        def sub(r, start, size=None):
            return [r[0] + start, r[0] + start + size if size else r[1]]

        r = sub(u_region, 0)
        u_hi = [place(f"u_hi{i}", [P, UB, TOK], F32R, at=r) for i in range(3)]
        u_lo = [place(f"u_lo{i}", [P, UB, TOK], F32R, at=r) for i in range(3)]
        r = sub(u_region, 0)
        f_hi = place("f_hi", [P, 8, TOK], F32R, at=r)
        f_lo = place("f_lo", [P, 8, TOK], F32R, at=r)
        r = sub(u_region, 0)
        xn = place("xn", [P, NT, D], at=r)
        mod32 = [place(f"mod32_{i}", [P, 4, P], at=r) for i in range(2)]
        ln_g = place("ln_g", [P, D], at=r)
        ln_b = place("ln_b", [P, D], at=r)
        first_raw = [place(f"first_raw{i}", [P, KB, P], at=r) for i in range(FIRST_RING)]
        mask32 = place("mask32", [P, 2, P], at=sub(t_region, 0))
        res = place("res", [P, NT, D], at=sub(x_region, 0))
        y32 = place("y32", [P, KB, TOK], at=sub(x_region, 0))
        r = sub(t_region, 0)
        gated = [place(f"gated{i}", [P, TOK], at=r) for i in range(2)]
        value = [place(f"value{i}", [P, TOK], at=r) for i in range(2)]
        prod = place("prod", [P, TOK], at=r)
        y_out = gated
        c_rows = place("c_rows", [P, 2, D], at=r)
        junk = place("junk", [P, D], at=r)
        r = sub(x_region, 0)
        apad = [place(f"apad{i}", [P, PW], at=r) for i in range(2)]
        sums = [place(f"sums{i}", [P, PW], at=r) for i in range(2)]
        inv = [place(f"inv{i}", [P, PW], at=r) for i in range(2)]
        pool_u = place("pool_u", [P, TOK], at=r)
        r = sub(t_region, 0)
        pu_hi = [place(f"pu_hi{i}", [P, TOK], F32R, at=r) for i in range(2)]
        pu_lo = [place(f"pu_lo{i}", [P, TOK], F32R, at=r) for i in range(2)]
        pool_y = [place(f"pool_y{i}", [P, TOK], at=r) for i in range(2)]
        ig = place("ig", [ROWS, TOK], at=r)
        fg = place("fg", [ROWS, TOK], at=r)
        kT = place("kT", [P, TOK], at=r)
        r = sub(x_region, 0)
        cos = place("cos", [P, SEQ], at=r)
        sin = place("sin", [P, SEQ], at=r)
        qT = [place(f"qT{i}", [P, TOK], at=r) for i in range(2)]
        vT = place("vT", [P, TOK], at=r)
        vaug = place("vaug", [P, NT, 2, AH + 1], at=r)
        rope_c = place("rope_c", [P, SEQ], at=r)
        rope_s = place("rope_s", [P, SEQ], at=r)
        r = sub(t_region, 0)
        probs = [place(f"probs{i}", [P, 5, P], at=r) for i in range(2)]
        probsT = [place(f"probsT{i}", [P, 5, P], at=r) for i in range(2)]
        att = place("att", [P, NT, P], at=r)
        mx = place("mx", [P, 4, 2], at=r)
        mrow = place("mrow", [P, 4], at=r)
        negm = place("negm", [P, 4], at=r)
        esink = place("esink", [P, 4], at=r)
        den = place("den", [P, 2], at=r)
        rden = place("rden", [P, 2], at=r)
        r = sub(x_region, 0)
        r_i = place("r_i", [ROWS, TOK], at=r)
        r_a = place("r_a", [ROWS, TOK], at=r)
        r_b = place("r_b", [ROWS, TOK], at=r)
        r_m = place("r_m", [ROWS, TOK], at=r)
        r_t = place("r_t", [ROWS, TOK], at=r)
        r_w = place("r_w", [ROWS, TOK], at=r)
        zeros = place("zeros", [ROWS, P], at=r)
        m_in = place("m_in", [ROWS, NT + 1], at=r)
        r_dec = place("r_dec", [ROWS, NT], at=r)
        r_e = place("r_e", [ROWS, TOK], at=sub(u_region, UB * TOK * 4))
        n_row = [place(f"n_row{i}", [ROWS, TOK], at=sub(u_region, (4 * UB + i) * TOK * 4)) for i in range(4)]
        r = sub(t_region, 0)
        neg_m = place("neg_m", [ROWS, TOK], at=r)
        cols = place("cols", [P, NT, 4, ROWS], at=r)
        decay = place("decay", [P, 2 * HEADS, NT], at=r)
        hwork = place("hwork", [P, NT, HD], at=r)
        hstat = place("hstat", [P, NT, 6], at=r)
        haggr = place("haggr", [P, NT, 2], at=r)
        hrstd = place("hrstd", [P, NT], at=r)
        hroot = place("hroot", [P, NT], at=r)
        denr = [place(f"denr{i}", [P, 2], at=r) for i in range(2)]
        rdenr = [place(f"rdenr{i}", [P, 2], at=r) for i in range(2)]
        total = [place(f"total{i}", [P, 2, HD + 1], at=r) for i in range(2)]
        state = place("state", [P, NT, 2, HD + 1], at=r)
        inter = [place(f"inter{i}", [P, 2, HD + 1], at=r) for i in range(2)]
        vw = [place(f"vw{i}", [P, HD + 1], at=r) for i in range(2)]
        odd_k = place("odd_k", [P, TOK], at=r)
        r = sub(x_region, 0)
        hq = [place(f"hq{i}", [P, TOK], at=r) for i in range(2)]
        hk = [place("even_k", [P, TOK], at=r), odd_k]
        hv = place("hv", [P, TOK], at=r)
        ho = place("ho", [P, TOK], at=r)
        k_tok = place("k_tok", [P, NT, P], at=r)
        v_tok = place("v_tok", [P, NT, HD + 1], at=r)
        wexp = [place(f"wexp{i}", [P, 2, P], at=r) for i in range(2)]

        ps = stack.enter_context(nc.psum_tensor("ps", [P, 8, 512], F32))
        spill = nc.dram_tensor("res_spill", [TOK, D], F32, kind="Internal").ap()

        raw_full = [sem("raw_full0"), sem("raw_full1")]
        first_full = [sem(f"first_full{i}") for i in range(FIRST_RING)]
        mod_full = [sem("mod_full0"), sem("mod_full1")]
        hi_done = sem("hi_done")
        lo_done = [sem("lo_done0"), sem("lo_done1")]
        mod_pe, mod_done = sem("mod_pe"), sem("mod_done")
        blk_done, blk_out = sem("blk_done"), sem("blk_out")
        phase = sem("phase")
        c_in = [sem("c_in0"), sem("c_in1")]
        late_in = sem("late_in")
        c_ready = sem("c_ready")
        const_in, tab_in = sem("const_in"), sem("tab_in")
        inv_in = [sem("inv_in0"), sem("inv_in1")]
        x_in = [sem(f"x_in{i}") for i in range(NT)]
        stored = sem("stored")
        a_step, v_step = sem("a_step"), sem("v_step")
        mod_ready = sem("mod_ready")
        var_done, root_done = sem("var_done"), sem("root_done")
        stat_done, normed = sem("stat_done"), sem("normed")
        xn_ready = sem("xn_ready")
        gained = sem("gained")
        x_new = sem("x_new")
        xt_done, xt_act = sem("xt_done"), sem("xt_act")
        h_ready = sem("h_ready")
        pu_ready, pu_used, py_free = sem("pu_ready"), sem("pu_used"), sem("py_free")
        q_done, q_out = sem("q_done"), sem("q_out")
        rot_done, rope_done = sem("rot_done"), sem("rope_done")
        vt_done, vt_evac = sem("vt_done"), sem("vt_evac")
        s_done, s_max, p_exp, pt_done, pt_evac, pv_done, pv_evac = (
            sem(n) for n in ("s_done", "s_max", "p_exp", "pt_done", "pt_evac", "pv_done", "pv_evac"))
        at_done, at_evac = sem("at_done"), sem("at_evac")
        row_act, row_dve, row_pe, row_evac = (sem(n) for n in ("row_act", "row_dve", "row_pe", "row_evac"))
        kt_done, kt_evac, v_evac = sem("kt_done"), sem("kt_evac"), sem("v_evac")
        vw_done, st_done, st_step = sem("vw_done"), sem("st_done"), sem("st_step")
        e_done, e_exp, w_done, n_done, i_evac, n_add = (
            sem(n) for n in ("e_done", "e_exp", "w_done", "n_done", "i_evac", "n_add"))
        past_done = sem("past_done")
        hr_ready, hr_done, hr_evac = sem("hr_ready"), sem("hr_done"), sem("hr_evac")
        u_split = sem("u_split")
        pair_free = sem("pair_free")
        room = sem("room")
        y_split = sem("y_split")
        f_split = sem("f_split")
        tr_done, tr_free = sem("tr_done"), sem("tr_free")

        block = stack.enter_context(nc.Block())

        def live(l):
            return LATENT if l == DEPTH - 1 else ALL

        def tiles_of(l):
            return LT if l == DEPTH - 1 else NT

        def over(eng, c):
            eng.drain().then_inc(phase, 1)
            eng.wait_ge(phase, c.next(phase, 3))

        def arrive(eng, c):
            eng.drain().then_inc(phase, 1)
            c.next(phase, 3)

        def scan_index(direction, chunk):
            if direction == 0:
                return (NT - LT) + chunk if chunk < LT else chunk - LT
            return NT - 1 - chunk

        def chunk_at(direction, s):
            return next(k for k in range(NT) if scan_index(direction, k) == s)

        def units(l):
            return [(p, i, x) for p in range(PAIRS) for i in range(tiles_of(l)) for x in range(2)]

        def beside_units(l):
            def queries(q, at, each):
                return {at + k: ("queries", q, (each * k, each * (k + 1))) for k in range(PART // each)}

            if l < DEPTH - 1:
                return {0: ("outputs", 1, range(LT, NT)), **queries(0, 1, 6), 5: ("turn",), **queries(1, 6, 8),
                        9: ("outputs", 0, range(0, LT))}
            return {0: ("outputs", 1, range(0, LT)), **queries(0, 1, 6), 5: ("turn",)}

        def band(i):
            return [j for j in (i - 1, i, i + 1) if 0 <= j < LT] if i < LT else []

        def keys(i):
            b = band(i)
            return [(j, n) for n, j in enumerate(b + list(range(LT, NT)))]

        def head_shares(l):
            lt = tiles_of(l)
            marks = [0, 6]
            for _ in range(NT - 1):
                marks.append(marks[-1] + 3)
            for _ in range(lt):
                marks.append(marks[-1] + (9 if l == 0 else 14))
            assert marks[-1] < 4 * PART
            return marks + [4 * PART]

        def head_ends(l, place_):
            marks = head_shares(l)
            return [j for j in range(4) if marks[place_] < PART * (j + 1) <= marks[place_ + 1]]

        STATES = [(s, d) for s in range(NT - 1) for d in range(2)]

        @block.sync
        def _(sp):
            c = Count()

            def load_pair(n, blocks, first=False, m=None, mods=0):
                for j in range(2):
                    if not first:
                        sp.wait_ge(lo_done[j], c.next(lo_done[j], 2))
                    width = blocks[j] * P
                    sp.dma_start(raw[j][:].rearrange("p k m -> p (k m)")[:, 0:width],
                                 w_tiles[n + j, :, 0:width]).then_inc(raw_full[j], 16)
                    if j == 0:
                        for k in range(mods):
                            load_mod(m + k, (mod_slot[0] + k) % 2)
                        mod_slot[0] += mods

            mod_slot = [0]

            def load_mod(m, slot, first=False):
                if not first:
                    sp.wait_ge(mod_done, c.next(mod_done))
                sp.dma_start(mod_raw[slot][:].rearrange("p k m -> p (k m)"), w_mod[m]).then_inc(mod_full[slot], 16)

            def run(n, pairs, blocks, m=None, mods=0):
                with sp.Fori(0, pairs // 2) as i:
                    c.enter(i, {lo_done[0]: 4, lo_done[1]: 4, mod_done: 2 * mods})
                    for k in range(2):
                        load_pair(n + 4 * i + 2 * k, blocks, m=None if m is None else m + mods * (2 * i + k), mods=mods)
                    c.leave(pairs // 2)
                return n + 2 * pairs

            for m in range(KB):
                for k, used in enumerate((mod_pe, mod_done)):
                    slot = (2 * m + k) % FIRST_RING
                    if 2 * m >= FIRST_RING:
                        sp.wait_ge(used, m - FIRST_RING // 2 + 1)
                    sp.dma_start(first_raw[slot][:].rearrange("p k m -> p (k m)"), w_mod[KB * k + m]).then_inc(
                        first_full[slot], 16)
            load_pair(0, (KB, KB), first=True)
            m = MODS_FIRST
            for j in range(2):
                load_mod(m + j, j, first=True)
            c.next(mod_done, KB)
            load_pair(2, (KB, KB))
            m += 2
            n = run(4, (IN_TILES - 4) // 2, (KB, KB))
            n = run(n, 2, (KB, UB))
            n = run(n, 3 * KB - 2, (KB, UB), m, 1)
            m += 3 * KB - 2
            load_pair(n, (KB, KB))
            n = run(n + 2, (DEPTH * MB - m) // 2, (KB, KB), m, 2)
            load_pair(n, (KB, KB))
            n += 2
            for l in range(DEPTH):
                if l:
                    n = run(n, IN_TILES // 2, (KB, KB))
                    n = run(n, 3 * KB, (KB, UB))
                last = (l + 1) * LAYER_TILES - KB
                n = run(n, (last - n) // 2, (KB, KB))
                n = run(n, KB // 2, (FG[-1], FG[-1]))

        @block.gpsimd
        def _(pool):
            c = Count()

            def low_halves(tiles):
                with pool.Fori(0, tiles // 2) as i:
                    c.enter(i, {hi_done: 4, lo_done[0]: 2, lo_done[1]: 2})
                    for j in range(2):
                        for part in (slice(0, HALF), slice(HALF, KB)):
                            pool.wait_ge(hi_done, c.next(hi_done))
                            nc.gpsimd.tensor_tensor(w_lo[j][:, part, :], raw[j][:, part, :],
                                                    w_hi[j][:, part, :].bitcast(F32),
                                                    ALU.subtract).then_inc(lo_done[j], c.sig(lo_done[j]))
                    c.leave(tiles // 2)

            def gain(n_t):
                pool.wait_ge(tab_in, c.next(tab_in, 32))
                for t in range(n_t):
                    pool.wait_ge(normed, c.next(normed))
                    nc.gpsimd.tensor_tensor(res[:, t, :], res[:, t, :], ln_g[:], ALU.mult).then_inc(
                        gained, c.sig(gained))

            at_ = 0
            for l in range(DEPTH):
                for upto in (l * LAYER_TILES + IN_TILES + 7 * KB + 2, min((l + 1) * LAYER_TILES + 2, DEPTH * LAYER_TILES)):
                    low_halves(upto - at_)
                    at_ = upto
                    if upto == l * LAYER_TILES + IN_TILES + 7 * KB + 2:
                        c.next(tab_in, 32)
                    gain(tiles_of(l))

        @block.tensor
        def _(pe):
            c = Count()

            def cut(slot):
                pe.wait_ge(lo_done[slot], c.next(lo_done[slot]))

            def product(slot, buf, k_blocks, rhs, chunks, w0=0, fresh=True, spare=1, parts=None,
                        k_ready=None, only=None):
                begin, end = parts or (0, 3 * k_blocks)
                if begin == 0 and not only:
                    if fresh:
                        cut(slot)
                    free = c.now(blk_done, spare)
                    if not isinstance(free, int) or free > 0:
                        pe.wait_ge(blk_out, free)
                a_hi, a_lo = rhs
                pairs = ((w_hi, a_hi), (w_hi, a_lo), (w_lo, a_hi))
                for n in range(begin, end):
                    k, (w, a) = n // 3, pairs[n % 3]
                    if k_ready is not None and n % 3 == 0:
                        k_ready(k)
                    if n == 3 * HALF and not only:
                        cut(slot)
                    for q, (t0, size) in enumerate(chunks):
                        if only not in (None, q):
                            continue
                        mm = nc.tensor.matmul(ps[:, 2 * buf + q, 0:size], w[slot][:, w0 + k, :],
                                              a[:, k, t0:t0 + size], start=n == 0, stop=n == 3 * k_blocks - 1)
                if end == 3 * k_blocks and only in (None, len(chunks) - 1):
                    if k_blocks <= HALF and fresh:
                        c.next(lo_done[slot])
                    mm.then_inc(blk_done, c.sig(blk_done))

            def modulation(tile, full, out_ap):
                pe.wait_ge(full, c.next(full, 16))
                for k in range(KB):
                    mm = nc.tensor.matmul(out_ap, tile[:, k, :], cact[:, k, :],
                                          start=(k == 0), stop=(k == KB - 1))
                mm.then_inc(mod_pe, c.sig(mod_pe))

            def norm_turns(l):
                for t in range(tiles_of(l)):
                    pe.wait_ge(xn_ready, c.next(xn_ready))
                    for half in range(2):
                        if c.now(xt_done) >= 2:
                            pe.wait_ge(xt_act, c.now(xt_done, 1))
                        for k in range(4):
                            mm = nc.tensor.transpose(ps[:, 4 + half, k * P:(k + 1) * P],
                                                     xn[:, t, (4 * half + k) * P:(4 * half + k + 1) * P], ident[:])
                        mm.then_inc(xt_done, c.sig(xt_done))

            def first_two(b, chunks, short=0):
                turned = c.now(xt_done)
                for q, (t0, size) in enumerate(chunks):
                    after = sum(n for _, n in chunks[q + 1:])
                    pe.wait_ge(h_ready, turned - 2 * (after + short) // P)
                    for j in range(2):
                        product(j, (b + j) % 2, KB, (h_hi, h_lo), chunks, spare=1 - j, only=q)

            def turn_back(par, chunks):
                pe.wait_ge(tr_free, c.now(tr_done, -1))
                for q, (t0, size) in enumerate(chunks):
                    for t in range(size // P):
                        mm = nc.tensor.transpose(ps[:, 4 + 2 * par + q, t * P:(t + 1) * P],
                                                 y_out[par][:, t0 + t * P:t0 + (t + 1) * P], ident[:])
                mm.then_inc(tr_done, c.sig(tr_done))

            pe.wait_ge(a_step, 1)
            c.next(a_step)
            for m in range(KB):
                slot = 2 * m % FIRST_RING
                modulation(first_raw[slot], first_full[slot], ps[:, 6, 2 * m:2 * m + 2])
            pe.wait_ge(const_in, CONST_ALL)
            pe.wait_ge(late_in, LATE_ALL)
            norm_turns(0)
            arrive(pe, c)
            for l in range(DEPTH):
                chunks = live(l)
                lt = tiles_of(l)
                b0 = c.now(blk_done)
                first_two(b0, chunks, TOK - lt * P)
                for g in range(2, UB):
                    product(g % 2, (b0 + g) % 2, KB, (h_hi, h_lo), chunks)
                if l:
                    pe.wait_ge(h_ready, c.now(xt_done))
                product(0, (b0 + UB) % 2, KB, (h_hi, h_lo), ALL)
                for g in range(UB):
                    if g == 2:
                        product(0, (b0 + UB + 3) % 2, KB, (h_hi, h_lo), ALL)
                    pe.wait_ge(pu_ready, c.next(pu_ready))
                    product(1, (b0 + UB + 1 + g + g // 2) % 2, 1, (pu_hi[g % 2][:].unsqueeze(1), pu_lo[g % 2][:].unsqueeze(1)),
                            chunks, w0=g, fresh=(g == 0))
                arrive(pe, c)

                b = c.now(blk_done)
                product(1, b % 2, KB, (h_hi, h_lo), ALL)

                def rotate(z, bank):
                    nc.tensor.matmul(ps[:, bank, 0:SEQ], rot[:], z[:, 0:SEQ], start=True,
                                     stop=True).then_inc(rot_done, c.sig(rot_done))

                def queries(p, q, bank, parts=(0, PART)):
                    t0, size = chunks[q]
                    pairs = ((w_hi, h_hi), (w_hi, h_lo), (w_lo, h_hi))
                    for n in range(*parts):
                        k, (w, a) = n // 3, pairs[n % 3]
                        if q == 0 and n % (3 * HALF) == 0:
                            cut(p % 2)
                        mm = nc.tensor.matmul(ps[:, bank, 0:size], w[p % 2][:, k, :], a[:, k, t0:t0 + size],
                                              start=n == 0, stop=n == PART - 1)
                    if parts[1] == PART:
                        mm.then_inc(q_done, c.sig(q_done))

                pe.wait_ge(blk_out, c.now(blk_done, 1))
                rotate(kT, 4)
                for q in range(len(chunks)):
                    queries(0, q, 2 * ((b + 1) % 2) + q)
                pe.wait_ge(blk_out, c.now(blk_done))
                for t in range(NT):
                    mm = nc.tensor.transpose(ps[:, 6 + t // 4, (t % 4) * P:(t % 4 + 1) * P],
                                             vT[:, t * P:(t + 1) * P], ident[:])
                mm.then_inc(vt_done, c.sig(vt_done))
                pe.wait_ge(rope_done, c.now(rot_done))
                pe.wait_ge(q_out, c.now(q_done))
                rotate(qT[0], 4)
                pe.wait_ge(vt_evac, c.next(vt_evac))
                pe.wait_ge(rope_done, c.now(rot_done))
                U = units(l)
                first = c.now(s_done)
                per_pair = 2 * lt
                plan = beside_units(l)

                def scores(n):
                    p, i, x = U[n]
                    rows = slice(AH * x, AH * x + AH)
                    bank = 2 + 2 * (n % 2)
                    if first + n >= 2:
                        pe.wait_ge(p_exp, first + n - 1)
                    q = qT[p % 2][rows, i * P:(i + 1) * P]
                    b = band(i)
                    if b:
                        width = len(b) * P
                        edge = [(n_, mask16[:, 0 if j < i else 1, :]) for n_, j in enumerate(b) if j != i]
                        nc.tensor.matmul(ps[:, bank, 0:width], q, kT[rows, b[0] * P:(b[-1] + 1) * P],
                                         start=True, stop=not edge)
                        for e, (n_, mask) in enumerate(edge):
                            nc.tensor.matmul(ps[:, bank, n_ * P:(n_ + 1) * P], ident16[:], mask,
                                             start=False, stop=e == len(edge) - 1)
                    nc.tensor.matmul(ps[:, bank + 1, 0:CTX], q, kT[rows, SEQ:TOK], start=True,
                                     stop=True).then_inc(s_done, c.sig(s_done))

                def turn_probs(n):
                    i = U[n][1]
                    pe.wait_ge(p_exp, first + n + 1)
                    if first + n:
                        pe.wait_ge(pt_evac, first + n)
                    for j, place_ in keys(i):
                        mm = nc.tensor.transpose(ps[:, 6 + place_ // 4, (place_ % 4) * P:(place_ % 4 + 1) * P],
                                                 probs[n % 2][:, place_, :], ident[:])
                    mm.then_inc(pt_done, c.sig(pt_done))

                def weigh_values(n):
                    _, i, x = U[n]
                    pe.wait_ge(pt_evac, first + n + 1)
                    if first + n:
                        pe.wait_ge(pv_evac, first + n)
                    for m_, (j, place_) in enumerate(keys(i)):
                        mm = nc.tensor.matmul(ps[:, 1, 0:AH + 1], probsT[n % 2][:, place_, :], vaug[:, j, x, :],
                                              start=(m_ == 0), stop=(m_ == len(keys(i)) - 1))
                    mm.then_inc(pv_done, c.sig(pv_done))

                def turn_outputs(n, tiles):
                    pe.wait_ge(pv_evac, first + n)
                    for k, t in enumerate(tiles):
                        mm = nc.tensor.transpose(ps[:, 0, k * P:(k + 1) * P], att[:, t, :], ident[:])
                    mm.then_inc(at_done, c.sig(at_done))

                def beside_unit(n):
                    p, job = n // per_pair, plan.get(n % per_pair)
                    if job is None:
                        return
                    if job[0] == "outputs":
                        if p >= job[1]:
                            pe.wait_ge(q_out, c.now(q_done))
                            turn_outputs(n, job[2])
                    elif p + 1 < PAIRS:
                        if job[0] == "turn":
                            pe.wait_ge(q_out, c.now(q_done))
                            rotate(qT[(p + 1) % 2], 0)
                        else:
                            if job[2][0] == 0:
                                if c.now(at_done):
                                    pe.wait_ge(at_evac, c.now(at_done))
                                pe.wait_ge(rope_done, c.now(rot_done))
                            queries(p + 1, job[1], 0, job[2])

                scores(0)
                scores(1)
                turn_probs(0)
                for n in range(len(U)):
                    if n + 2 < len(U):
                        if n % per_pair == per_pair - 2:
                            pe.wait_ge(rope_done, c.now(rot_done))
                        scores(n + 2)
                    if n + 1 < len(U):
                        turn_probs(n + 1)
                    beside_unit(n)
                    weigh_values(n)
                if c.now(at_done):
                    pe.wait_ge(at_evac, c.now(at_done))
                turn_outputs(len(U), plan[0][2])
                pe.wait_ge(at_evac, c.now(at_done))
                arrive(pe, c)

                head_b = c.now(blk_done)
                marks = head_shares(l)
                head_chunks = (chunks, ALL, ALL, chunks)

                def head_product(j, parts=None, spare=1):
                    product(j % 2, (head_b + j) % 2, KB, (h_hi, h_lo), head_chunks[j], spare=spare, parts=parts)

                def beside(hd, place_):
                    if hd + 1 < HEADS:
                        for j in range(4):
                            begin, end = (min(max(m - PART * j, 0), PART) for m in marks[place_:place_ + 2])
                            if begin < end:
                                head_product(j, (begin, end))

                head_product(0)
                head_product(1)
                pe.wait_ge(row_dve, c.next(row_dve, 2))
                for t in range(NT):
                    for q in range(4):
                        at_ = ((t % 3) * 4 + q) * ROWS
                        nc.tensor.transpose(ps[:, 4 + t // 3, at_:at_ + ROWS], n_row[q][:, t * P:(t + 1) * P],
                                            ident[0:ROWS, 0:ROWS])
                for d in range(2):
                    for hd in range(HEADS):
                        row, at_ = 32 * d + hd, (HEADS * d + hd) * NT
                        mm = nc.tensor.matmul(ps[:, 6, at_:at_ + NT], ident[0:ROWS, row:row + 1].broadcast_to([ROWS, P]),
                                              r_dec[:], start=True, stop=True)
                mm.then_inc(row_pe, c.sig(row_pe))
                head_product(2)
                head_product(3)
                pe.wait_ge(row_evac, c.next(row_evac))
                for hd in range(HEADS):
                    pe.wait_ge(blk_out, head_b + 4 * hd + 3)
                    for src, bank in ((hk[hd % 2], 6), (hv, 4)):
                        for t in range(NT):
                            mm = nc.tensor.transpose(ps[:, bank + t // 4, (t % 4) * P:(t % 4 + 1) * P],
                                                     src[:, t * P:(t + 1) * P], ident[:])
                        mm.then_inc(kt_done, c.sig(kt_done))
                    first = c.now(e_done)

                    def decays(t):
                        if t >= 2:
                            pe.wait_ge(w_done, first + t - 1)
                        bank = 4 + t % 2
                        nc.tensor.matmul(ps[:, bank, 0:2 * P], ident16[:], mask16[:].rearrange("p a b -> p (a b)"),
                                         start=True, stop=False)
                        for d in range(2):
                            row = 32 * d + hd
                            nc.tensor.matmul(ps[:, bank, d * P:(d + 1) * P],
                                             ident[0:ROWS, row:row + 1].broadcast_to([ROWS, P]),
                                             neg_m[:, t * P:(t + 1) * P], start=False, stop=d == 1)
                        nc.tensor.matmul(ps[:, bank, 2 * P:3 * P], hk[hd % 2][:, t * P:(t + 1) * P],
                                         hq[hd % 2][:, t * P:(t + 1) * P],
                                         start=True, stop=True).then_inc(e_done, c.sig(e_done))

                    def past(t):
                        if first + t:
                            pe.wait_ge(i_evac, first + t)
                        for d in range(2):
                            mm = nc.tensor.matmul(ps[:, 7, d * (HD + 1):(d + 1) * (HD + 1)],
                                                  hq[hd % 2][:, t * P:(t + 1) * P],
                                                  state[:, scan_index(d, t), d, :], start=True, stop=True)
                        mm.then_inc(past_done, c.sig(past_done))

                    beside(hd, 0)
                    pe.wait_ge(kt_evac, c.next(kt_evac))
                    pe.wait_ge(v_evac, c.next(v_evac))
                    decays(0)
                    decays(1)
                    for s, d in STATES:
                        pe.wait_ge(vw_done, c.next(vw_done))
                        if c.now(st_done) >= 2:
                            pe.wait_ge(st_step, c.now(st_done, 1))
                        nc.tensor.matmul(ps[:, 6 + d, 0:HD + 1], k_tok[:, chunk_at(d, s), :], vw[d][:],
                                         start=True, stop=True).then_inc(st_done, c.sig(st_done))
                        if d == 1:
                            beside(hd, 1 + s)
                    pe.wait_ge(st_step, c.now(st_done))
                    past(0)
                    for t in range(lt):
                        if t + 1 < lt:
                            past(t + 1)
                        beside(hd, NT + t)
                        pe.wait_ge(w_done, first + t + 1)
                        if first + t:
                            pe.wait_ge(n_add, first + t)
                        for d in range(2):
                            mm = nc.tensor.matmul(ps[:, 6, d * (HD + 1):(d + 1) * (HD + 1)], wexp[t % 2][:, d, :],
                                                  v_tok[:, t, :], start=True, stop=True)
                        mm.then_inc(n_done, c.sig(n_done))
                        if t + 2 < lt:
                            decays(t + 2)
                    beside(hd, NT + lt)
                    pe.wait_ge(hr_ready, c.next(hr_ready))
                    for t in range(lt):
                        mm = nc.tensor.transpose(ps[:, 4 + t // 4, (t % 4) * P:(t % 4 + 1) * P], hwork[:, t, :], ident[:])
                    mm.then_inc(hr_done, c.sig(hr_done))
                    pe.wait_ge(hr_evac, c.next(hr_evac))
                arrive(pe, c)

                pe.wait_ge(u_split, c.next(u_split, HEADS))
                b = c.now(blk_done)
                with pe.Fori(0, KB // 2) as i:
                    c.enter(i, {lo_done[0]: 12, lo_done[1]: 12, blk_done: 12})
                    for pr in range(6):
                        product(0, b % 2, KB, (h_hi, h_lo), chunks)
                        product(1, (b + 1) % 2, UB, (u_hi[pr % 3], u_lo[pr % 3]), chunks)
                    c.leave(KB // 2)
                arrive(pe, c)

                merged = c.next(y_split, KB)

                def projection(k_blocks, a_hi, a_lo, k_ready=None):
                    b = c.now(blk_done)

                    def block_(j, k_ready=None):
                        product(j, (b + j) % 2, k_blocks, (a_hi, a_lo), chunks, k_ready=k_ready)

                    def turn(j, back):
                        pe.wait_ge(blk_out, c.now(blk_done, back))
                        turn_back(j, chunks)

                    block_(0, k_ready)
                    with pe.Fori(0, KB // 2 - 1) as i:
                        c.enter(i, {lo_done[0]: 2, lo_done[1]: 2, blk_done: 2, tr_done: 2})
                        for j in range(2):
                            block_(1 - j)
                            turn(j, 1)
                        c.leave(KB // 2 - 1)
                    block_(1)
                    turn(0, 1)
                    turn(1, 0)

                projection(KB, h_hi, h_lo, lambda k: pe.wait_ge(y_split, merged - KB + 1 + k))
                arrive(pe, c)
                norm_turns(l)
                arrive(pe, c)

                for g, blocks in enumerate(FG):
                    b = c.now(blk_done)
                    if g == 0:
                        first_two(b, chunks)
                        for j in range(2, 4):
                            product(j % 2, (b + j) % 2, KB, (h_hi, h_lo), chunks)
                    passes = blocks // 2 - (g == 0)
                    with pe.Fori(0, passes) as i:
                        c.enter(i, {lo_done[0]: 4, lo_done[1]: 4, blk_done: 4})
                        for j in range(4):
                            product(j % 2, (b + j) % 2, KB, (h_hi, h_lo), chunks)
                        c.leave(passes)
                    split = c.next(f_split, blocks)
                    projection(blocks, f_hi, f_lo, lambda k: pe.wait_ge(f_split, split - blocks + 1 + k))
                arrive(pe, c)
                if l == 0:
                    norm_turns(0)
                    arrive(pe, c)

        @block.scalar
        def _(act):
            c = Count()

            def link(ins):
                ins.then_inc(a_step, c.sig(a_step))
                act.wait_ge(a_step, c.now(a_step))

            def table(func):
                link(nc.scalar.activation(idle[:], ident[:, 0:1], func))

            def high(slot):
                act.wait_ge(raw_full[slot], c.next(raw_full[slot], 16))
                for part in (slice(0, HALF), slice(HALF, KB)):
                    nc.scalar.activation(w_hi[slot][:, part, :], raw[slot][:, part, :], ACT.Copy).then_inc(
                        hi_done, c.sig(hi_done))

            def take(pieces, slot=None):
                act.wait_ge(blk_done, c.next(blk_done))
                if slot is not None:
                    high(slot)
                for n, piece in enumerate(pieces):
                    ins = piece()
                ins.then_inc(blk_out, c.sig(blk_out))

            def copy_out(dst, buf, chunks, func=ACT.Copy, rows=slice(0, P), **kw):
                return [lambda q=q, t0=t0, size=size: nc.scalar.activation(
                    dst[rows, t0:t0 + size], ps[rows, 2 * buf + q, 0:size], func, **kw)
                    for q, (t0, size) in enumerate(chunks)]

            def roots(n_t):
                table(ACT.Sqrt)
                act.wait_ge(var_done, c.next(var_done))
                nc.scalar.activation(root[:, 0:n_t], aggr[:, 0:n_t, 1], ACT.Sqrt, bias=eps[:]).then_inc(
                    root_done, c.sig(root_done))

            def modulated(l, shift, scale):
                n_t = NT if shift == SHIFT1 else tiles_of(l)
                roots(n_t)
                if l and shift == SHIFT1:
                    for t in range(tiles_of(l)):
                        act.dma_start(spill[t * P:(t + 1) * P, :], res[:, t, :]).then_inc(stored, 16)
                if l == 0 and shift == SHIFT1:
                    act.wait_ge(mod_ready, 1)
                for t in range(n_t):
                    s = 0 if t < LT else 1
                    for half in range(2):
                        act.wait_ge(xt_done, c.next(xt_done))
                        if c.now(xt_act) >= 2:
                            act.wait_ge(h_ready, c.now(xt_act, 1))
                        for k in range(4):
                            kk = 4 * half + k
                            ins = nc.scalar.activation(mod32[half][:, k, :], ps[:, 4 + half, k * P:(k + 1) * P],
                                                       ACT.Identity, scale=modv[l][:, scale + kk, s:s + 1],
                                                       bias=modv[l][:, shift + kk, s:s + 1])
                        ins.then_inc(xt_act, c.sig(xt_act))

            def post_norm(n_t):
                roots(n_t)
                act.wait_ge(stat_done, c.next(stat_done))
                for t in range(n_t):
                    nc.scalar.activation(res[:, t, :], res[:, t, :], ACT.Identity, scale=rstd[:, t:t + 1],
                                         bias=nmr[:, t:t + 1]).then_inc(normed, c.sig(normed))
                c.next(x_new, n_t)

            def load_x(l):
                for t in range(tiles_of(l)):
                    if l == 0:
                        src = x_lat[t * P:(t + 1) * P, :] if t < LT else ctx[(t - LT) * P:(t - LT + 1) * P, :]
                    else:
                        src = spill[t * P:(t + 1) * P, :]
                    act.dma_start(res[:, t, :], src).then_inc(x_in[t], 16)

            def load_gb(l, which):
                act.dma_start(ln_g[:], ln_gb[l, which:which + 1, :].partition_broadcast(P)).then_inc(tab_in, 16)
                act.dma_start(ln_b[:], ln_gb[l, which + 1:which + 2, :].partition_broadcast(P)).then_inc(tab_in, 16)

            def condition_rows(times):
                act.wait_ge(c_in[1], 16 * times)
                nc.scalar.activation(c_rows[:], c_rows[:], ACT.Silu).then_inc(c_ready, 1)

            act.dma_start(cin[:], cvec).then_inc(c_in[0], 16)
            act.dma_start(c_rows[:].rearrange("p a b -> p (a b)"), c_lines.partition_broadcast(P)).then_inc(c_in[1], 16)
            for dst, src in ((bmod, b_mod), (ident, consts[0]), (mask32, consts[2:4].rearrange("a p b -> p a b")),
                             (sink, sinks)):
                act.dma_start(dst[:], src).then_inc(const_in, 16)
            load_x(0)
            for dst, src in ((vec, vecs), (ifb, ifbias), (rot, consts[1])):
                act.dma_start(dst[:], src).then_inc(late_in, 16)
            act.wait_ge(c_in[0], 16)
            nc.scalar.activation(cact[:], cin[:], ACT.Silu).then_inc(a_step, c.sig(a_step))
            condition_rows(1)
            act.wait_ge(const_in, CONST_ALL)
            high(0)
            high(1)
            modulated(0, SHIFT1, SCALE1)
            act.wait_ge(late_in, LATE_ALL)
            over(act, c)
            for l in range(DEPTH):
                chunks = live(l)
                lt = tiles_of(l)
                width = chunks[-1][0] + chunks[-1][1]
                b0 = c.now(blk_out)
                if l:
                    act.wait_ge(stored, c.next(stored, 16 * lt))
                for g in range(2):
                    act.dma_start(inv[g][:], pool_inv[g:g + 1, :].partition_broadcast(P)).then_inc(inv_in[g], 16)
                if l:
                    act.drain().then_inc(room, 1)
                for g in range(UB):
                    if g >= 2:
                        act.wait_ge(pu_ready, c.now(pu_ready) + g - 1)
                        act.dma_start(inv[g % 2][:], pool_inv[g:g + 1, :].partition_broadcast(P)).then_inc(inv_in[g % 2], 16)
                    buf = (b0 + g) % 2
                    a = apad[g % 2]
                    pieces = [lambda buf=buf, a=a: nc.scalar.activation(a[:, LAT0:LAT0 + SEQ], ps[:, 2 * buf, 0:SEQ], ACT.Copy)]
                    if len(chunks) > 1:
                        pieces.append(lambda buf=buf, a=a: nc.scalar.activation(a[:, CTX0:CTX0 + CTX], ps[:, 2 * buf + 1, 0:CTX], ACT.Copy))
                    if g == 0:
                        act.wait_ge(py_free, c.next(py_free))
                    take(pieces, g % 2)
                c.next(pu_ready, UB)
                buf = (b0 + UB) % 2
                take([lambda q=q, t0=t0, size=size, dst=dst, r0=r0, j=j, buf=buf: nc.scalar.activation(
                    dst[:, t0:t0 + size], ps[r0:r0 + ROWS, 2 * buf + q, 0:size], ACT.Identity, bias=ifb[:, l, j:j + 1])
                    for j, (dst, r0) in enumerate(((ig, 0), (fg, 64))) for q, (t0, size) in enumerate(ALL)], 0)
                for g in range(UB):
                    if g == 2:
                        take(copy_out(kT, (b0 + UB + 3) % 2, ALL))
                    if g >= 2:
                        act.wait_ge(py_free, c.now(py_free) + g - 1)
                    take(copy_out(pool_y[g % 2], (b0 + UB + 1 + g + g // 2) % 2, chunks, scale=vec[:, l, 0, g:g + 1]),
                         1 if g == UB - 1 else None)
                high(0)
                c.next(py_free, UB)
                over(act, c)

                act.dma_start(cos[:], tables[0]).then_inc(tab_in, 16)
                act.dma_start(sin[:], tables[1]).then_inc(tab_in, 16)
                b = c.now(blk_out)
                take(copy_out(vT, b % 2, ALL), 1)

                def queries_out(p, q, bank):
                    t0, size = chunks[q]
                    act.wait_ge(q_done, c.next(q_done))
                    if q == len(chunks) - 1:
                        high(p % 2)
                    nc.scalar.activation(qT[p % 2][:, t0:t0 + size], ps[:, bank, 0:size], ACT.Copy).then_inc(
                        q_out, c.sig(q_out))

                for q in range(len(chunks)):
                    queries_out(0, q, 2 * ((b + 1) % 2) + q)
                U = units(l)
                first = c.now(p_exp)
                plan = beside_units(l)

                def exponentials(n):
                    p, i, x = U[n]
                    par, q4, bank = n % 2, n % 4, 2 + 2 * (n % 2)
                    nb = len(band(i))
                    act.wait_ge(s_max, first + n + 1)
                    if first + n >= 4:
                        act.wait_ge(pv_evac, first + n - 3)
                    if nb:
                        nc.scalar.activation(probs[par][:, 0:nb, :].rearrange("p a b -> p (a b)"),
                                             ps[:, bank, 0:nb * P], ACT.Exp, scale=AH ** -0.5, bias=negm[:, q4:q4 + 1])
                    head = p + PAIRS * x
                    nc.scalar.activation(esink[:, q4:q4 + 1], negm[:, q4:q4 + 1], ACT.Exp,
                                         bias=sink[:, l, head:head + 1])
                    nc.scalar.activation(probs[par][:, nb:nb + 2, :].rearrange("p a b -> p (a b)"),
                                         ps[:, bank + 1, 0:CTX], ACT.Exp, scale=AH ** -0.5,
                                         bias=negm[:, q4:q4 + 1]).then_inc(p_exp, c.sig(p_exp))

                table(ACT.Exp)
                exponentials(0)
                exponentials(1)
                for n, (p, i, x) in enumerate(U):
                    par = n % 2
                    nk = len(keys(i))
                    act.wait_ge(pt_done, first + n + 1)
                    if first + n >= 2:
                        act.wait_ge(pv_done, first + n - 1)
                    ins = nc.scalar.activation(probsT[par][:, 0:min(nk, 4), :].rearrange("p a b -> p (a b)"),
                                               ps[:, 6, 0:min(nk, 4) * P], ACT.Copy)
                    if nk > 4:
                        ins = nc.scalar.activation(probsT[par][:, 4, :], ps[:, 7, 0:P], ACT.Copy)
                    ins.then_inc(pt_evac, c.sig(pt_evac))
                    if n + 2 < len(U):
                        exponentials(n + 2)
                    job = plan.get(n % (2 * lt), ("",))
                    if p + 1 < PAIRS and job[0] == "queries" and job[2][1] == PART:
                        queries_out(p + 1, job[1], 0)
                over(act, c)

                link(nc.scalar.activation(r_t[:], fg[:], ACT.Abs))
                link(nc.scalar.activation(r_a[:], r_t[:], ACT.Exp, scale=-1.0))
                nc.scalar.activation(r_b[:], r_a[:], ACT.Ln, bias=1.0).then_inc(row_act, c.sig(row_act))
                act.wait_ge(blk_done, c.next(blk_done))
                high(0)
                act.wait_ge(row_dve, c.next(row_dve))
                nc.scalar.activation(r_dec[:], r_dec[:], ACT.Exp)
                nc.scalar.activation(r_t[:], r_t[:], ACT.Exp)
                nc.scalar.activation(r_w[:], r_w[:], ACT.Exp)
                nc.scalar.activation(r_e[:], r_e[:], ACT.Exp, scale=-1.0).then_inc(row_act, c.sig(row_act))
                c.next(row_dve)
                act.wait_ge(blk_done, c.next(blk_done))
                high(1)
                act.wait_ge(row_evac, c.next(row_evac))
                b = c.now(blk_out)

                def head_out(hd, j):
                    buf = (b + j) % 2
                    return (lambda: copy_out(hq[hd % 2], buf, chunks),
                            lambda: copy_out(hk[hd % 2], buf, ALL, scale=HD ** -0.5),
                            lambda: copy_out(hv, buf, ALL),
                            lambda: copy_out(ho, buf, chunks, ACT.Sigmoid))[j]()

                for j in range(2):
                    for piece in head_out(0, j):
                        ins = piece()
                    ins.then_inc(blk_out, c.sig(blk_out))
                take(head_out(0, 2), 0)
                take(head_out(0, 3), 1)

                def next_head(hd, place_):
                    if hd + 1 < HEADS:
                        for j in head_ends(l, place_):
                            if j < 3:
                                take(head_out(hd + 1, j), j % 2)
                            else:
                                act.wait_ge(blk_done, c.next(blk_done))
                                high(1)
                                table(ACT.Sigmoid)
                                act.wait_ge(hr_evac, c.next(hr_evac))
                                for piece in head_out(hd + 1, j):
                                    ins = piece()
                                ins.then_inc(blk_out, c.sig(blk_out))

                for hd in range(HEADS):
                    act.wait_ge(kt_done, c.next(kt_done))
                    nc.scalar.activation(k_tok[:, 0:4, :].rearrange("p a b -> p (a b)"), ps[:, 6, :], ACT.Copy)
                    nc.scalar.activation(k_tok[:, 4:6, :].rearrange("p a b -> p (a b)"), ps[:, 7, 0:2 * P],
                                         ACT.Copy).then_inc(kt_evac, c.sig(kt_evac))
                    act.wait_ge(kt_done, c.next(kt_done))
                    first = c.now(e_exp)

                    def decay_out(t):
                        act.wait_ge(e_done, c.next(e_done))
                        if first + t >= 2:
                            act.wait_ge(n_done, first + t - 1)
                        for d in range(2):
                            row = 32 * d + hd
                            ins = nc.scalar.activation(wexp[t % 2][:, d, :], ps[:, 4 + t % 2, d * P:(d + 1) * P], ACT.Exp,
                                                       bias=cols[:, t, 0, row:row + 1])
                        ins.then_inc(e_exp, c.sig(e_exp))

                    def past_out(t):
                        act.wait_ge(past_done, c.next(past_done))
                        if first + t >= 2:
                            act.wait_ge(n_add, first + t - 1)
                        for d in range(2):
                            row = 32 * d + hd
                            ins = nc.scalar.activation(inter[t % 2][:, d, :], ps[:, 7, d * (HD + 1):(d + 1) * (HD + 1)],
                                                       ACT.Copy, scale=cols[:, t, 2, row:row + 1])
                        ins.then_inc(i_evac, c.sig(i_evac))

                    table(ACT.Exp)
                    decay_out(0)
                    decay_out(1)
                    for place_ in range(NT):
                        next_head(hd, place_)
                    past_out(0)
                    for t in range(lt):
                        if t + 1 < lt:
                            past_out(t + 1)
                        if t + 2 < lt:
                            decay_out(t + 2)
                        next_head(hd, NT + t)
                    table(ACT.Sqrt)
                    act.wait_ge(var_done, c.next(var_done))
                    nc.scalar.activation(hroot[:, 0:lt], haggr[:, 0:lt, 1], ACT.Sqrt, bias=eps[:]).then_inc(
                        root_done, c.sig(root_done))
                    next_head(hd, NT + lt)
                over(act, c)
                c.next(hr_evac)

                if l == 0:
                    act.dma_start(c_rows[:].rearrange("p a b -> p (a b)"), c_lines.partition_broadcast(P)).then_inc(
                        c_in[1], 16)
                    condition_rows(2)
                b = c.now(blk_out)
                with act.Fori(0, KB // 2) as i:
                    c.enter(i, {blk_done: 12, blk_out: 12, raw_full[0]: 96, raw_full[1]: 96, hi_done: 24, a_step: 1, pair_free: 6})
                    table(ACT.Sigmoid)
                    for pr in range(6):
                        par = pr % 2
                        act.wait_ge(pair_free, c.next(pair_free))
                        take(copy_out(gated[par], b % 2, chunks, ACT.Sigmoid), 0)
                        take(copy_out(value[par], (b + 1) % 2, chunks), 1)
                    c.leave(KB // 2)
                over(act, c)

                act.wait_ge(y_split, c.next(y_split, KB))
                load_x(l)

                def projection(gate, end=False):
                    b = c.now(blk_out)

                    def two(i, ahead=True):
                        for j in range(2):
                            buf = (b + j) % 2
                            pieces = [lambda q=q, t0=t0, size=size, j=j, buf=buf: nc.scalar.activation(
                                y_out[j][:, t0:t0 + size], ps[:, 2 * buf + q, 0:size], ACT.Copy,
                                scale=gate_col(i * 2 + (gate + j), q)) for q, (t0, size) in enumerate(chunks)]
                            take(pieces, j if ahead else None)

                    def gate_col(m, q):
                        return modv[l][:, bass.ds(m, 1), q]

                    turns = KB // 2 - (1 if end else 0)
                    with act.Fori(0, turns) as i:
                        c.enter(i, {blk_done: 2, blk_out: 2, raw_full[0]: 16, raw_full[1]: 16, hi_done: 4})
                        two(i)
                        c.leave(turns)
                    if end:
                        two(turns, ahead=False)

                projection(GATE1)
                over(act, c)
                load_gb(l, 0)
                post_norm(lt)
                modulated(l, SHIFT2, SCALE2)
                over(act, c)
                for g, blocks in enumerate(FG):
                    b = c.now(blk_out)
                    with act.Fori(0, blocks // 2) as i:
                        c.enter(i, {blk_done: 4, blk_out: 4, raw_full[0]: 32, raw_full[1]: 32, hi_done: 8, a_step: 1, pair_free: 2})
                        table(ACT.Silu)
                        for j in range(2):
                            act.wait_ge(pair_free, c.next(pair_free))
                            take(copy_out(gated[j], b % 2, chunks, ACT.Silu), 0)
                            take(copy_out(value[j], (b + 1) % 2, chunks), 1)
                        c.leave(blocks // 2)
                    last_group = l == DEPTH - 1 and g == len(FG) - 1
                    projection(GATE2, end=last_group)
                over(act, c)
                load_gb(l, 2)
                post_norm(lt)
                if l == 0:
                    modulated(1, SHIFT1, SCALE1)
                    over(act, c)
            for t in range(LT):
                act.wait_ge(x_new, c.now(x_new) - LT + t + 1)
                act.dma_start(out[t * P:(t + 1) * P, :], res[:, t, :]).then_inc(stored, 16)
            act.wait_ge(stored, c.next(stored, 16 * LT))

        @block.vector
        def _(dve):
            c = Count()
            v = nc.vector

            def link(ins):
                ins.then_inc(v_step, c.sig(v_step))
                dve.wait_ge(v_step, c.now(v_step))

            def sums_of(t):
                for half in range(2):
                    ins = v.bn_stats(stats[:, t, half, :], res[:, t, half * 512:(half + 1) * 512])
                return ins

            def block_sums(i, n_t):
                for t in range(n_t):
                    ins = v.bn_stats(stats[:, t, bass.ds(i, 1), :].rearrange("p a b -> p (a b)"),
                                     res[:, t, bass.ds(i * P, P)])
                return ins

            def deviations(n_t, last, groups=2):
                if last is not None:
                    link(last)
                for t in range(n_t):
                    ins = v.bn_aggr(aggr[:, t, :], stats[:, t, 0:groups, :].rearrange("p a b -> p (a b)"))
                ins.then_inc(var_done, c.sig(var_done))
                dve.wait_ge(var_done, c.now(var_done))
                dve.wait_ge(root_done, c.next(root_done))
                link(v.reciprocal(rstd[:, 0:n_t], root[:, 0:n_t]))

            def halves(t):
                for half in range(2):
                    dve.wait_ge(xt_act, c.next(xt_act))
                    hi = h_hi[:, 4 * half:4 * half + 4, t * P:(t + 1) * P]
                    link(v.tensor_copy(hi, mod32[half][:]))
                    v.tensor_tensor(h_lo[:, 4 * half:4 * half + 4, t * P:(t + 1) * P], mod32[half][:],
                                    hi.bitcast(F32), ALU.subtract).then_inc(h_ready, c.sig(h_ready))

            def modulated(n_t, last, first=False):
                deviations(n_t, last)

                def normalised(t):
                    v.tensor_scalar(xn[:, t, :], res[:, t, :], aggr[:, t, 0:1], rstd[:, t:t + 1], ALU.subtract,
                                    ALU.mult).then_inc(xn_ready, c.sig(xn_ready))

                if first:
                    dve.wait_ge(mod_pe, KB)
                    v.tensor_tensor(modv[0][:, 0:KB, :], ps[:, 6, 0:2 * KB].rearrange("p (a b) -> p a b", b=2),
                                    bmod[:, 0, 0:KB].unsqueeze(2).broadcast_to([P, KB, 2]), ALU.add).then_inc(mod_ready, 1)
                normalised(0)
                for t in range(n_t):
                    if t + 1 < n_t:
                        normalised(t + 1)
                    halves(t)

            def modulation(layer, m, slot, tile=None, full=None):
                tile, full = tile or mod_raw[slot], full or mod_full[slot]
                dve.wait_ge(full, c.next(full, 16))
                w = tile[:].rearrange("p k m -> p (k m)")
                link(v.tensor_tensor_reduce(junk[:], w, c_rows[:, 0, :], 1.0, 0.0, ALU.mult, ALU.add,
                                            mod_sum[:, slot, 0:1]))
                v.tensor_tensor_reduce(junk[:], w, c_rows[:, 1, :], 1.0, 0.0, ALU.mult, ALU.add,
                                       mod_sum[:, slot, 1:2]).then_inc(mod_done, c.sig(mod_done))
                dve.wait_ge(mod_done, c.now(mod_done))
                link(v.tensor_scalar(modv[layer][:, bass.ds(m, 1), :], mod_sum[:, slot:slot + 1, :],
                                     bmod[:, layer, bass.ds(m, 1)], None, ALU.add))

            MODULATION = {mod_full[0]: 16, mod_full[1]: 16, mod_done: 2}

            def post_norm(n_t):
                deviations(n_t, None, groups=KB)
                v.scalar_tensor_tensor(nmr[:, 0:n_t], aggr[:, 0:n_t, 0], -1.0, rstd[:, 0:n_t], ALU.mult,
                                       ALU.mult).then_inc(stat_done, c.sig(stat_done))
                dve.wait_ge(tab_in, c.next(tab_in, 32))

                def biased(t):
                    dve.wait_ge(gained, c.next(gained))
                    v.tensor_tensor(res[:, t, :], res[:, t, :], ln_b[:], ALU.add).then_inc(x_new, c.sig(x_new))

                biased(0)
                for t in range(n_t):
                    if t + 1 < n_t:
                        biased(t + 1)
                    dve.wait_ge(x_new, c.now(x_new, 1 if t + 1 < n_t else 0))
                    ins = sums_of(t)
                return ins

            dve.wait_ge(const_in, CONST_ALL)
            v.memset(eps[:], EPS)
            v.tensor_copy(ident16[:], ident[:])
            v.tensor_copy(mask16[:], mask32[:])
            v.tensor_scalar(negsink[:], sink[:], -1.0, None, ALU.mult)
            for first in (SCALE1, SCALE2):
                ins = v.tensor_scalar(bmod[:, :, first:first + KB], bmod[:, :, first:first + KB], 1.0, None, ALU.add)
            link(ins)
            dve.wait_ge(c_ready, 1)
            for t in range(KB):
                slot = (2 * t + 1) % FIRST_RING
                modulation(0, KB + t, t % 2, first_raw[slot], first_full[slot])
                if t < NT:
                    dve.wait_ge(x_in[t], c.next(x_in[t], 16))
                    link(sums_of(t))
            dve.wait_ge(late_in, LATE_ALL)
            modulated(NT, None, first=True)
            dve.drain().then_inc(pair_free, c.sig(pair_free, 2))
            dve.drain().then_inc(tr_free, c.sig(tr_free, 2))
            over(dve, c)
            for l in range(DEPTH):
                chunks = live(l)
                lt = tiles_of(l)
                tok = lt * P
                width = PW if len(chunks) > 1 else LATW
                segments = [(0, SEQ, LAT0), (SEQ, CTX, CTX0)][:len(chunks)]

                if l:
                    dve.wait_ge(room, 1)
                v.memset(apad[0][:], 0.0)
                v.memset(apad[1][:], 0.0).then_inc(py_free, c.sig(py_free))
                dve.wait_ge(py_free, c.now(py_free))
                products = c.now(blk_out) + UB + 1
                for g in range(UB):
                    w = WINDOWS[g]
                    a = apad[g % 2]
                    dve.wait_ge(blk_out, c.next(blk_out))
                    dve.wait_ge(inv_in[g % 2], c.next(inv_in[g % 2], 16))
                    src = a
                    for k in range(g + 1):
                        dst = sums[k % 2]
                        n = width - (2 ** (k + 1) - 1)
                        link(v.tensor_tensor(dst[:, 0:n], src[:, 0:n], src[:, 2 ** k:2 ** k + n], ALU.add))
                        src = dst
                    mean = sums[(g + 1) % 2]
                    n = width - 2 * PAD
                    link(v.tensor_tensor(mean[:, PAD:PAD + n], src[:, PAD - w // 2:PAD - w // 2 + n],
                                         inv[g % 2][:, PAD:PAD + n], ALU.mult))
                    for t0, size, at_ in segments:
                        ins = v.tensor_tensor(pool_u[:, t0:t0 + size], mean[:, at_:at_ + size], a[:, at_:at_ + size],
                                              ALU.subtract)
                    link(ins)
                    if g >= 2:
                        dve.wait_ge(blk_out, products + g - 1)
                    link(v.tensor_copy(pu_hi[g % 2][:, 0:tok], pool_u[:, 0:tok]))
                    v.tensor_tensor(pu_lo[g % 2][:, 0:tok], pool_u[:, 0:tok], pu_hi[g % 2][:, 0:tok].bitcast(F32),
                                    ALU.subtract).then_inc(pu_ready, c.sig(pu_ready))
                c.next(blk_out)
                for g in range(UB):
                    dve.wait_ge(blk_out, c.next(blk_out, 2 if g == 2 else 1))
                    hi = u_hi[0][:, g, 0:tok]
                    link(v.tensor_copy(hi, pool_y[g % 2][:, 0:tok]))
                    v.tensor_tensor(u_lo[0][:, g, 0:tok], pool_y[g % 2][:, 0:tok], hi.bitcast(F32),
                                    ALU.subtract).then_inc(py_free, c.sig(py_free))
                over(dve, c)

                v.memset(vaug[:, :, :, AH:AH + 1], 1.0)
                dve.wait_ge(tab_in, c.next(tab_in, 32))

                def rotated(z, bank):
                    dve.wait_ge(rot_done, c.next(rot_done))
                    v.tensor_tensor(rope_c[:], z[:, 0:SEQ], cos[:], ALU.mult)
                    link(v.tensor_tensor(rope_s[:], ps[:, bank, :], sin[:], ALU.mult))
                    v.tensor_tensor(z[:, 0:SEQ], rope_c[:], rope_s[:], ALU.add).then_inc(rope_done, c.sig(rope_done))

                rotated(kT, 4)
                dve.wait_ge(vt_done, c.next(vt_done))
                v.tensor_copy(vaug[:, 0:4, :, 0:AH], ps[:, 6, :].rearrange("p (a b d) -> p a b d", a=4, b=2))
                v.tensor_copy(vaug[:, 4:6, :, 0:AH], ps[:, 7, 0:2 * P].rearrange(
                    "p (a b d) -> p a b d", a=2, b=2)).then_inc(vt_evac, c.sig(vt_evac))
                dve.wait_ge(rope_done, c.now(rope_done))
                rotated(qT[0], 4)
                U = units(l)
                plan = beside_units(l)

                def maxima(n):
                    p, i, x = U[n]
                    q4, bank = n % 4, 2 + 2 * (n % 2)
                    head = p + PAIRS * x
                    nb = len(band(i))
                    dve.wait_ge(s_done, c.next(s_done))
                    m = mx[:, q4, 1:2]
                    if nb:
                        v.reduce_max(mx[:, q4, 0:1], ps[:, bank, 0:nb * P], AX_X)
                    link(v.reduce_max(m, ps[:, bank + 1, 0:CTX], AX_X))
                    if nb:
                        link(v.tensor_tensor(mrow[:, q4:q4 + 1], mx[:, q4, 0:1], m, ALU.max))
                        m = mrow[:, q4:q4 + 1]
                    v.tensor_scalar(negm[:, q4:q4 + 1], m, -(AH ** -0.5), negsink[:, l, head:head + 1],
                                    ALU.mult, ALU.min).then_inc(s_max, c.sig(s_max))

                def output(n):
                    _, i, x = U[n]
                    par, q4 = n % 2, n % 4
                    dve.wait_ge(pv_done, c.next(pv_done))
                    link(v.tensor_tensor(den[:, par:par + 1], ps[:, 1, AH:AH + 1], esink[:, q4:q4 + 1], ALU.add))
                    link(v.reciprocal(rden[:, par:par + 1], den[:, par:par + 1]))
                    v.tensor_scalar(att[:, i, AH * x:AH * x + AH], ps[:, 1, 0:AH], rden[:, par:par + 1], None,
                                    ALU.mult).then_inc(pv_evac, c.sig(pv_evac))

                def outputs_split(p, tiles):
                    dve.wait_ge(at_done, c.next(at_done))
                    ts = slice(tiles[0] * P, (tiles[-1] + 1) * P)
                    turned = ps[:, 0, 0:len(tiles) * P]
                    link(v.tensor_copy(u_hi[2][:, p, ts], turned))
                    v.tensor_tensor(u_lo[2][:, p, ts], turned, u_hi[2][:, p, ts].bitcast(F32),
                                    ALU.subtract).then_inc(at_evac, c.sig(at_evac))

                maxima(0)
                maxima(1)
                for n, (p, _, _) in enumerate(U):
                    if n + 2 < len(U):
                        maxima(n + 2)
                    job = plan.get(n % (2 * lt), ("",))
                    if job[0] == "outputs" and p >= job[1]:
                        outputs_split(p - job[1], job[2])
                    elif job[0] == "turn" and p + 1 < PAIRS:
                        dve.wait_ge(rope_done, c.now(rope_done))
                        rotated(qT[(p + 1) % 2], 0)
                    output(n)
                outputs_split(PAIRS - 1, plan[0][2])
                over(dve, c)

                def reorder(dst, src, back=False, by=None):
                    for rows, rev in ((slice(0, 32), False), (slice(32, ROWS), True)):
                        for natural, scan in ((slice(SEQ, TOK), slice(0, CTX)), (slice(0, SEQ), slice(CTX, TOK))):
                            a_, b_ = (scan, natural) if back else (natural, scan)
                            s_ = src[rows, a_]
                            if rev:
                                s_ = s_[:, ::-1]
                            if by is None:
                                ins = v.tensor_copy(dst[rows, b_], s_)
                            else:
                                ins = v.tensor_scalar(dst[rows, b_], s_, by, None, ALU.mult)
                    return ins

                v.memset(zeros[:], 0.0)
                v.memset(m_in[:, 0:1], 0.0)
                dve.wait_ge(row_act, c.next(row_act))
                link(v.scalar_tensor_tensor(r_m[:], fg[:], 0.0, r_b[:], ALU.min, ALU.subtract))
                reorder(r_i, ig)
                link(reorder(r_w, r_m))
                for s in range(NT):
                    cs = slice(s * P, (s + 1) * P)
                    ins = v.tensor_tensor_scan(r_b[:, cs], r_w[:, cs], zeros[:], 0.0, ALU.add, ALU.add)
                link(ins)
                link(v.tensor_tensor(r_a[:], r_i[:], r_b[:], ALU.subtract))
                for s in range(NT):
                    cs = slice(s * P, (s + 1) * P)
                    end = slice((s + 1) * P - 1, (s + 1) * P)
                    link(v.tensor_tensor_scan(r_m[:, cs], r_a[:, cs], r_a[:, cs], m_in[:, s:s + 1], ALU.max, ALU.max))
                    link(v.tensor_tensor(m_in[:, s + 1:s + 2], r_b[:, end], r_m[:, end], ALU.add))

                def by_chunk(r):
                    return r[:].rearrange("p (a b) -> p a b", b=P)

                ends = by_chunk(r_m)[:, :, P - 1:P]
                v.tensor_tensor(r_dec[:].unsqueeze(2), m_in[:, 0:NT].unsqueeze(2), ends, ALU.subtract)
                v.tensor_tensor(by_chunk(r_t), m_in[:, 0:NT].unsqueeze(2).broadcast_to([ROWS, NT, P]), by_chunk(r_m),
                                ALU.subtract)
                v.tensor_tensor(by_chunk(r_w), by_chunk(r_a), ends.broadcast_to([ROWS, NT, P]), ALU.subtract)
                v.tensor_tensor(r_e[:], r_b[:], r_m[:], ALU.add).then_inc(row_dve, c.sig(row_dve))
                reorder(n_row[0], r_a, back=True)
                reorder(neg_m, r_m, back=True, by=-1.0)
                dve.wait_ge(row_act, c.next(row_act))
                for q, r_ in ((1, r_w), (2, r_t), (3, r_e)):
                    ins = reorder(n_row[q], r_, back=True)
                ins.then_inc(row_dve, c.sig(row_dve))
                dve.wait_ge(row_pe, c.next(row_pe))
                for half in range(2):
                    v.tensor_copy(cols[:, 3 * half:3 * half + 3, :, :].rearrange("p a b d -> p (a b d)"),
                                  ps[:, 4 + half, 0:12 * ROWS])
                v.tensor_copy(decay[:].rearrange("p a b -> p (a b)"), ps[:, 6, 0:2 * HEADS * NT]).then_inc(
                    row_evac, c.sig(row_evac))
                dve.wait_ge(row_evac, c.now(row_evac))
                v.memset(v_tok[:, :, HD:HD + 1], 1.0)
                link(v.memset(state[:, 0, :, :], 0.0))
                for hd in range(HEADS):
                    dve.wait_ge(kt_done, c.next(kt_done, 2))
                    v.tensor_copy(v_tok[:, 0:4, 0:HD], ps[:, 4, :].rearrange("p (a b) -> p a b", b=HD))
                    v.tensor_copy(v_tok[:, 4:6, 0:HD], ps[:, 5, 0:2 * HD].rearrange("p (a b) -> p a b", b=HD)).then_inc(
                        v_evac, c.sig(v_evac))
                    dve.wait_ge(v_evac, c.now(v_evac))

                    def gated_v(n):
                        s, d = STATES[n]
                        t = chunk_at(d, s)
                        if n >= 2:
                            dve.wait_ge(st_done, c.now(st_done) + n - 1)
                        row = 32 * d + hd
                        v.tensor_scalar(vw[d][:], v_tok[:, t, :], cols[:, t, 1, row:row + 1], None,
                                        ALU.mult).then_inc(vw_done, c.sig(vw_done))

                    gated_v(0)
                    gated_v(1)
                    for n, (s, d) in enumerate(STATES):
                        dve.wait_ge(st_done, c.now(st_done) + n + 1)
                        v.scalar_tensor_tensor(state[:, s + 1, d, :], state[:, s, d, :],
                                               decay[:, HEADS * d + hd, s:s + 1], ps[:, 6 + d, 0:HD + 1],
                                               ALU.mult, ALU.add).then_inc(st_step, c.sig(st_step))
                        if n + 2 < len(STATES):
                            gated_v(n + 2)
                        if n:
                            dve.wait_ge(st_step, c.now(st_step, 1))
                    dve.wait_ge(st_step, c.now(st_step))
                    c.next(st_done, len(STATES))

                    def decayed(t):
                        dve.wait_ge(e_exp, c.next(e_exp))
                        v.tensor_tensor(wexp[t % 2][:], wexp[t % 2][:],
                                        ps[:, 4 + t % 2, 2 * P:3 * P].unsqueeze(1).broadcast_to([P, 2, P]),
                                        ALU.mult).then_inc(w_done, c.sig(w_done))

                    decayed(0)
                    decayed(1)
                    for t in range(lt):
                        dve.wait_ge(n_done, c.next(n_done))
                        dve.wait_ge(i_evac, c.next(i_evac))
                        both, most, share = total[t % 2], denr[t % 2], rdenr[t % 2]
                        v.tensor_tensor(both[:], ps[:, 6, 0:2 * (HD + 1)].rearrange("p (a b) -> p a b", a=2),
                                        inter[t % 2][:], ALU.add).then_inc(n_add, c.sig(n_add))
                        dve.wait_ge(n_add, c.now(n_add))
                        nq = both[:, :, HD]
                        link(v.scalar_tensor_tensor(most[:], nq, -1.0, nq, ALU.mult, ALU.max))
                        link(v.tensor_tensor(most[:], most[:], cols[:, t, 3, hd:hd + 33:32], ALU.max))
                        link(v.reciprocal(share[:], most[:]))
                        link(v.tensor_scalar(hwork[:, t, :], both[:, 0, 0:HD], share[:, 0:1], None, ALU.mult))
                        link(v.scalar_tensor_tensor(hwork[:, t, :], both[:, 1, 0:HD], share[:, 1:2], hwork[:, t, :],
                                                    ALU.mult, ALU.add))
                        ins = v.bn_stats(hstat[:, t, :], hwork[:, t, :])
                        if t + 2 < lt:
                            decayed(t + 2)
                    link(ins)
                    for t in range(lt):
                        ins = v.bn_aggr(haggr[:, t, :], hstat[:, t, :])
                    ins.then_inc(var_done, c.sig(var_done))
                    dve.wait_ge(var_done, c.now(var_done))
                    dve.wait_ge(root_done, c.next(root_done))
                    link(v.reciprocal(hrstd[:, 0:lt], hroot[:, 0:lt]))
                    for t in range(lt):
                        ins = v.tensor_scalar(hwork[:, t, :], hwork[:, t, :], haggr[:, t, 0:1], hrstd[:, t:t + 1],
                                              ALU.subtract, ALU.mult)
                    ins.then_inc(hr_ready, c.sig(hr_ready))
                    dve.wait_ge(hr_done, c.next(hr_done))
                    done = hwork[:].rearrange("p a b -> p (a b)")
                    dve.wait_ge(blk_out, BLOCKS * l + 11 + 4 * (hd + 1))
                    for q, (t0, size) in enumerate(chunks):
                        ins = v.scalar_tensor_tensor(done[:, t0:t0 + size], ps[:, 4 + q, 0:size], vec[:, l, 1, hd:hd + 1],
                                                     ho[:, t0:t0 + size], ALU.mult, ALU.mult)
                    ins.then_inc(hr_evac, c.sig(hr_evac))
                    dve.wait_ge(hr_evac, c.now(hr_evac))
                    hi = u_hi[1][:, hd, 0:tok]
                    link(v.tensor_copy(hi, done[:, 0:tok]))
                    v.tensor_tensor(u_lo[1][:, hd, 0:tok], done[:, 0:tok], hi.bitcast(F32),
                                    ALU.subtract).then_inc(u_split, c.sig(u_split))
                over(dve, c)
                c.next(blk_out, 1 + 4 * HEADS)

                if l == 0:
                    dve.wait_ge(c_ready, 2)
                with dve.Fori(0, KB // 2) as i:
                    step = {blk_out: 12, pair_free: 6, v_step: 4}
                    if l == 0:
                        step.update({mod_full[0]: 48, mod_full[1]: 48, mod_done: 6, v_step: 4 + 12})
                    c.enter(i, step)
                    for pr in range(6):
                        if l == 0:
                            modulation(0, i * 6 + (MODS_FIRST + pr), pr % 2)
                        dve.wait_ge(blk_out, c.next(blk_out, 2))
                        y = y32[:, i * 2 + pr // 3, 0:tok]
                        to = y if pr % 3 == 0 else prod[:, 0:tok]
                        v.tensor_tensor(to, gated[pr % 2][:, 0:tok], value[pr % 2][:, 0:tok], ALU.mult).then_inc(
                            pair_free, c.sig(pair_free))
                        dve.wait_ge(pair_free, c.now(pair_free))
                        if pr % 3:
                            link(v.tensor_tensor(y, y, prod[:, 0:tok], ALU.add))
                    c.leave(KB // 2)
                for k in range(KB):
                    link(v.tensor_copy(h_hi[:, k, 0:tok], y32[:, k, 0:tok])) if k else None
                    if k == 0:
                        over(dve, c)
                        link(v.tensor_copy(h_hi[:, k, 0:tok], y32[:, k, 0:tok]))
                    v.tensor_tensor(h_lo[:, k, 0:tok], y32[:, k, 0:tok], h_hi[:, k, 0:tok].bitcast(F32),
                                    ALU.subtract).then_inc(y_split, c.sig(y_split))

                def residual(alpha, m0=None, layer=1, sums=False):
                    with dve.Fori(0, KB // 2) as i:
                        step = {tr_done: 2, tr_free: 2}
                        if m0 is not None:
                            step.update({**MODULATION, v_step: 4})
                        if sums:
                            step[v_step] = step.get(v_step, 0) + 2
                        c.enter(i, step)
                        for j in range(2):
                            if m0 is not None and j == 0:
                                for slot in range(2):
                                    modulation(layer, i * 2 + (m0 + slot), slot)
                            dve.wait_ge(tr_done, c.next(tr_done))
                            for q, (t0, size) in enumerate(chunks):
                                t_ = t0 // P
                                r_ = res[:, t_:t_ + size // P, bass.ds(i * (2 * P) + j * P, P)]
                                ins = v.scalar_tensor_tensor(
                                    r_, r_, alpha, ps[:, 4 + 2 * j + q, 0:size].rearrange("p (a b) -> p a b", b=P),
                                    ALU.mult, ALU.add)
                            ins.then_inc(tr_free, c.sig(tr_free))
                            if sums:
                                dve.wait_ge(tr_free, c.now(tr_free))
                                link(block_sums(i * 2 + j, lt))
                        c.leave(KB // 2)

                for t in range(lt):
                    dve.wait_ge(x_in[t], c.next(x_in[t], 16))
                residual(ALPHA, GATE2 if l == 0 else None, layer=0, sums=True)
                c.next(blk_out, KB)
                over(dve, c)
                modulated(lt, post_norm(lt))
                over(dve, c)

                for g, blocks in enumerate(FG):
                    with dve.Fori(0, blocks // 2) as i:
                        step = {blk_out: 4, pair_free: 2, f_split: 2, v_step: 2}
                        mods = l == 0 and g < 2
                        if mods:
                            step.update({mod_full[0]: 32, mod_full[1]: 32, mod_done: 4, v_step: 2 + 8})
                        c.enter(i, step)
                        for j in range(2):
                            if mods:
                                for slot in range(2):
                                    modulation(1, i * 4 + ((0 if g == 0 else 3 * KB) + 2 * j + slot), slot)
                            dve.wait_ge(blk_out, c.next(blk_out, 2))
                            v.tensor_tensor(prod[:, 0:tok], gated[j][:, 0:tok], value[j][:, 0:tok],
                                            ALU.mult).then_inc(pair_free, c.sig(pair_free))
                            dve.wait_ge(pair_free, c.now(pair_free))
                            hi = f_hi[:, i * 2 + j, 0:tok]
                            link(v.tensor_copy(hi, prod[:, 0:tok]))
                            v.tensor_tensor(f_lo[:, i * 2 + j, 0:tok], prod[:, 0:tok], hi.bitcast(F32),
                                            ALU.subtract).then_inc(f_split, c.sig(f_split))
                            dve.wait_ge(f_split, c.now(f_split))
                        c.leave(blocks // 2)
                    residual(ALPHA if g == 0 else 1.0, (2 * KB, 5 * KB)[g] if l == 0 and g < 2 else None,
                             sums=g == len(FG) - 1)
                    c.next(blk_out, KB)
                over(dve, c)
                last = post_norm(lt)
                if l == 0:
                    modulated(NT, last)
                    over(dve, c)


def constants():
    ident = np.eye(P, dtype=np.float32)
    rot = np.zeros((P, P), np.float32)
    for f in range(P):
        if f % 32 < 16:
            rot[f + 16, f] = -1.0
        else:
            rot[f - 16, f] = 1.0
    row, col = np.arange(P)[:, None], np.arange(P)[None, :]
    before = np.where(col < row, np.float32(MASKED), np.float32(0))
    after = np.where(col > row, np.float32(MASKED), np.float32(0))
    consts = np.stack([ident, rot, before, after]).astype(np.float32)
    grid_w, pairs = 64, AH // 4
    inv = np.float32(10000.0) ** (-np.arange(pairs, dtype=np.float32) / np.float32(pairs))
    t = np.arange(SEQ)
    axes = ((t // grid_w).astype(np.float32), (t % grid_w).astype(np.float32))
    ang = np.concatenate([np.concatenate([a[:, None] * inv] * 2, axis=1) for a in axes], axis=1).T
    ang = np.concatenate([ang, ang], axis=0).astype(np.float32)
    tables = np.stack([np.cos(ang), np.sin(ang)]).astype(np.float32)
    inverse = np.zeros((UB, PW), np.float32)
    for g, w in enumerate(WINDOWS):
        for n, at in ((SEQ, LAT0), (CTX, CTX0)):
            tt = np.arange(n)
            count = np.clip(tt - w // 2 + w, 0, n) - np.clip(tt - w // 2, 0, n)
            inverse[g, at:at + n] = np.float32(1) / count.astype(np.float32)
    return consts, tables, inverse


def blocks_of(w):
    k, m = w.shape[0] // P, w.shape[1] // P
    return w.reshape(k, P, m, P).transpose(2, 1, 0, 3).reshape(m, P, k * P)


def modulation_tiles(w_mod):
    tiles = np.concatenate([blocks_of(w) for w in w_mod])
    rows = w_mod.transpose(0, 2, 1).reshape(tiles.shape)
    return np.concatenate([tiles[:KB], rows[KB:]])


def widened(tiles):
    if tiles.shape[-1] == KB * P:
        return tiles
    out = np.zeros(tiles.shape[:-1] + (KB * P,), tiles.dtype)
    out[..., :tiles.shape[-1]] = tiles
    return out


def layer_tiles(w_in, pool_w, w_branch, w_out, w_gate, w_up, w_down):
    sizes = (BW, BW, BW, BW, BW, 2 * HEADS, 2 * HEADS, BW, P, P, 3 * D)
    a, q, k, v, o, ig, fg, qa, ka, va, gates = np.split(w_in, np.cumsum(sizes)[:-1], axis=1)
    rows = np.zeros((D, P), w_in.dtype)
    for n, part in enumerate((ig, fg)):
        for d in range(2):
            rows[:, 64 * n + 32 * d:64 * n + 32 * d + HEADS] = part[:, HEADS * d:HEADS * (d + 1)]
    qa = qa.reshape(D, 2, PAIRS, AH).transpose(0, 2, 1, 3).reshape(D, BW)
    tiles = [blocks_of(a), blocks_of(rows), widened(pool_w.transpose(1, 0, 2).reshape(1, P, UB * P)),
             blocks_of(ka), blocks_of(va), blocks_of(qa)]
    parts = [blocks_of(z) for z in (q, k, v, o)]
    tiles += [np.stack([z[h] for z in parts]) for h in range(HEADS)]
    branch = [w_branch[0], w_branch[1],
              w_branch[2].reshape(2, PAIRS, AH, D).transpose(1, 0, 2, 3).reshape(BW, D)]
    g = blocks_of(gates).reshape(3, KB, P, KB * P)
    b = np.stack([widened(blocks_of(z)) for z in branch])
    tiles += [np.stack([g, b], axis=2).transpose(1, 0, 2, 3, 4).reshape(6 * KB, P, KB * P)]
    tiles += [blocks_of(w_out)]
    gate, up = blocks_of(w_gate), blocks_of(w_up)
    at = 0
    for n in FG:
        tiles += [np.stack([gate[at:at + n], up[at:at + n]], axis=1).reshape(2 * n, P, KB * P),
                  widened(blocks_of(w_down[at * P:(at + n) * P]))]
        at += n
    return np.concatenate(tiles)


def by_partition(z):
    z = z.reshape(z.shape[:-1] + (-1, P))
    return np.ascontiguousarray(np.moveaxis(z, -1, 0))


def kernel(x, c, ctx, c_ctx, w_mod, b_mod, w_in, pool_w, pool_scale, m_b_i, m_b_f, m_norm_w, attn_sink, w_branch,
           w_out, ln1_g, ln1_b, ln2_g, ln2_b, w_ffn_gate, w_ffn_up, w_ffn_down):
    import concourse.bacc as bacc
    from concourse.bass_utils import run_bass_kernel_spmd

    a = {n: np.asarray(z) for n, z in dict(
        x=x, c=c, ctx=ctx, c_ctx=c_ctx, w_mod=w_mod, b_mod=b_mod, w_in=w_in, pool_w=pool_w, pool_scale=pool_scale,
        m_b_i=m_b_i, m_b_f=m_b_f, m_norm_w=m_norm_w, attn_sink=attn_sink, w_branch=w_branch, w_out=w_out,
        ln1_g=ln1_g, ln1_b=ln1_b, ln2_g=ln2_g, ln2_b=ln2_b, w_ffn_gate=w_ffn_gate, w_ffn_up=w_ffn_up,
        w_ffn_down=w_ffn_down).items()}
    consts, tables, inverse = constants()
    rows = np.zeros((ROWS, DEPTH, 2), np.float32)
    for n, bias in enumerate((a["m_b_i"], a["m_b_f"])):
        for d in range(2):
            rows[32 * d:32 * d + HEADS, :, n] = bias[:, d].T
    arrays = {
        "x_lat": a["x"].reshape(SEQ, D),
        "ctx": a["ctx"].reshape(CTX, D),
        "cvec": by_partition(np.stack([a["c"].reshape(D), a["c_ctx"]])).transpose(0, 2, 1),
        "c_lines": np.stack([a["c"].reshape(D), a["c_ctx"].reshape(D)]).reshape(1, 2 * D),
        "w_mod": modulation_tiles(a["w_mod"]),
        "b_mod": by_partition(a["b_mod"]),
        "w_tiles": np.concatenate([layer_tiles(*(a[n][l] for n in (
            "w_in", "pool_w", "w_branch", "w_out", "w_ffn_gate", "w_ffn_up", "w_ffn_down"))) for l in range(DEPTH)]),
        "vecs": by_partition(np.stack([a["pool_scale"], a["m_norm_w"]], axis=1)),
        "ifbias": rows,
        "sinks": np.ascontiguousarray(np.broadcast_to(a["attn_sink"].reshape(1, DEPTH, 8), (P, DEPTH, 8))),
        "ln_gb": np.stack([a["ln1_g"], a["ln1_b"], a["ln2_g"], a["ln2_b"]], axis=1),
        "consts": consts,
        "tables": tables,
        "pool_inv": inverse,
    }
    arrays = {n: np.ascontiguousarray(z) for n, z in arrays.items()}
    nc = bacc.Bacc("TRN2", target_bir_lowering=False, num_devices=1)
    args = {n: nc.dram_tensor(n, z.shape, mybir.dt.from_np(z.dtype), kind="ExternalInput").ap()
            for n, z in arrays.items()}
    out = nc.dram_tensor("out", (SEQ, D), F32, kind="ExternalOutput").ap()
    trunk(nc, out=out, **args)
    result = run_bass_kernel_spmd(nc, [arrays], core_ids=[0])
    return result.results[0]["out"].reshape(1, SEQ, D)
```
